# Optimizing a Trainium2 kernel written in Bass

```python
import math
import jax, jax.numpy as jnp
from jax import lax
import numpy as np

D_MODEL = 1024
BATCH = 1
SEQ = 512
DEPTH = 1

N_MIXERS = 3
EPS = 1e-6
ATTN_GROUPS = ((128, 1), (512, 4), (2048, 16))
ATTN_N_GROUPS = len(ATTN_GROUPS)
ATTN_HEADS_PER_GROUP = 8
ATTN_HEAD_DIM = 64
ATTN_BLOCK = 128
ATTN_GROUP_WIDTH = ATTN_HEADS_PER_GROUP * ATTN_HEAD_DIM
ATTN_IN_WIDTH = ATTN_N_GROUPS * 3 * ATTN_GROUP_WIDTH
CONV_CHANNELS = D_MODEL
CONV_WIDTH = 31
HGRN_EXPAND = 128
HGRN_HEADS = D_MODEL // HGRN_EXPAND
HGRN_KEY_DIM = HGRN_HEADS * HGRN_EXPAND
HGRN_HEAD_V = D_MODEL // HGRN_HEADS
HGRN_VALUE_DIM = HGRN_HEADS * HGRN_HEAD_V
HGRN_CHUNK = 64
FFN_HIDDEN = 2816
FFN_CONV_WIDTH = 3
N_ATTN_LAYERS = len(range(0, DEPTH, N_MIXERS))
N_CONV_LAYERS = len(range(1, DEPTH, N_MIXERS))
N_HGRN_LAYERS = len(range(2, DEPTH, N_MIXERS))


def rms_norm(x, gain):
    xf = x.astype(jnp.float32)
    y = xf * lax.rsqrt(jnp.mean(xf * xf, axis=-1, keepdims=True) + EPS)
    return (y * gain.astype(jnp.float32)).astype(x.dtype)

def layer_norm(x, gain, bias):
    xf = x.astype(jnp.float32)
    mu = jnp.mean(xf, axis=-1, keepdims=True)
    var = jnp.mean(jnp.square(xf - mu), axis=-1, keepdims=True)
    y = (xf - mu) * lax.rsqrt(var + EPS)
    return (y * gain.astype(jnp.float32) + bias.astype(jnp.float32)).astype(x.dtype)

def causal_depthwise_conv(x, w, b):
    K, C = w.shape
    y = lax.conv_general_dilated(
        x, w[:, None, :].astype(x.dtype), window_strides=(1,), padding=((K - 1, 0),),
        dimension_numbers=('NWC', 'WIO', 'NWC'), feature_group_count=C)
    return y + b.astype(x.dtype)

def dilated_window_attention(q, k, v, window, dilation):
    B, S, H, Dh = q.shape
    span = window // dilation
    unit = dilation * ATTN_BLOCK
    L = -(-S // unit) * unit
    n = L // dilation
    nb = n // ATTN_BLOCK

    def to_blocks(t):
        t = jnp.pad(t, ((0, 0), (0, L - S), (0, 0), (0, 0)))
        t = t.reshape(B, n, dilation, H, Dh).transpose(0, 2, 3, 1, 4)
        return t.reshape(B, dilation, H, nb, ATTN_BLOCK, Dh)

    def with_prev(t):
        prev = jnp.pad(t, ((0, 0), (0, 0), (0, 0), (1, 0), (0, 0), (0, 0)))[:, :, :, :-1]
        return jnp.concatenate([prev, t], axis=-2)

    qb = to_blocks(q)
    kw = with_prev(to_blocks(k))
    vw = with_prev(to_blocks(v))
    s = jnp.einsum('brhnqd,brhnkd->brhnqk', qb, kw).astype(jnp.float32)
    qi = jnp.arange(ATTN_BLOCK)[:, None]
    kj = jnp.arange(2 * ATTN_BLOCK)[None, :]
    dist = qi + ATTN_BLOCK - kj
    band = (dist >= 0) & (dist <= span)
    kpos = jnp.arange(nb)[:, None, None] * ATTN_BLOCK + kj[None] - ATTN_BLOCK
    mask = band[None] & (kpos >= 0)
    s = jnp.where(mask, s, -jnp.inf)
    lse = jax.nn.logsumexp(s, axis=-1)
    p = jnp.exp(s - lse[..., None])
    o = jnp.einsum('brhnqk,brhnkd->brhnqd', p.astype(v.dtype), vw)
    o = o.reshape(B, dilation, H, n, Dh).transpose(0, 3, 1, 2, 4).reshape(B, L, H, Dh)[:, :S]
    lse = lse.reshape(B, dilation, H, n).transpose(0, 3, 1, 2).reshape(B, L, H)[:, :S]
    return o, lse

def dilated_attention_mixer(h, w_in, q_gain, k_gain, w_out):
    B, S, _ = h.shape
    proj = (h @ w_in).reshape(B, S, ATTN_N_GROUPS, 3, ATTN_HEADS_PER_GROUP, ATTN_HEAD_DIM)
    scale = ATTN_HEAD_DIM ** -0.5
    outs, lses = [], []
    for g, (window, dilation) in enumerate(ATTN_GROUPS):
        q = rms_norm(proj[:, :, g, 0], q_gain[g]) * scale
        k = rms_norm(proj[:, :, g, 1], k_gain[g])
        o, lse = dilated_window_attention(q, k, proj[:, :, g, 2], window, dilation)
        outs.append(o)
        lses.append(lse)
    weights = jax.nn.softmax(jnp.stack(lses), axis=0)
    o = jnp.sum(weights[..., None] * jnp.stack(outs).astype(jnp.float32), axis=0)
    return o.astype(h.dtype).reshape(B, S, ATTN_GROUP_WIDTH) @ w_out

def conformer_conv_mixer(h, w_in, b_in, dw_w, dw_b, ln_g, ln_b, w_out, b_out):
    u = h @ w_in + b_in
    a, gate = jnp.split(u, 2, axis=-1)
    u = a * jax.nn.sigmoid(gate)
    u = causal_depthwise_conv(u, dw_w, dw_b)
    u = jax.nn.silu(layer_norm(u, ln_g, ln_b))
    return u @ w_out + b_out

def hgrn2_chunk_scan(q, k, v, log_f):
    B, S, H, K = q.shape
    V = v.shape[-1]
    C = HGRN_CHUNK
    n = S // C

    def chunks(t):
        return t.reshape(B, n, C, H, t.shape[-1]).transpose(1, 0, 3, 2, 4)

    qc, kc, vc = chunks(q), chunks(k), chunks(v)
    bc = jnp.cumsum(chunks(log_f), axis=-2)
    tri = jnp.tril(jnp.ones((C, C), dtype=bool))[:, :, None]

    def step(state, xs):
        q_, k_, v_, b_ = xs
        o_inter = jnp.einsum('bhtk,bhkv->bhtv', q_ * jnp.exp(b_), state)
        diff = b_[:, :, :, None, :] - b_[:, :, None, :, :]
        decay = jnp.where(tri, jnp.exp(jnp.where(tri, diff, 0.0)), 0.0)
        scores = jnp.einsum('bhtsk,bhsk->bhts', q_[:, :, :, None, :] * decay, k_)
        o_intra = jnp.einsum('bhts,bhsv->bhtv', scores, v_)
        b_last = b_[:, :, -1, :]
        k_dec = k_ * jnp.exp(b_last[:, :, None, :] - b_)
        state = state * jnp.exp(b_last)[..., None] + jnp.einsum('bhsk,bhsv->bhkv', k_dec, v_)
        return state, o_inter + o_intra

    state0 = jnp.zeros((B, H, K, V), jnp.float32)
    _, o = lax.scan(step, state0, (qc, kc, vc, bc))
    return o.transpose(1, 0, 3, 2, 4).reshape(B, S, H, V)

def hgrn2_mixer(h, w_in, lower_bound, norm_gain, w_out):
    B, S, _ = h.shape
    q, f, i, g = jnp.split(h @ w_in, [HGRN_KEY_DIM, 2 * HGRN_KEY_DIM,
                                      2 * HGRN_KEY_DIM + HGRN_VALUE_DIM], axis=-1)
    q = jax.nn.silu(q.astype(jnp.float32))
    lb = lower_bound.astype(jnp.float32)
    log_f = jnp.logaddexp(jnp.log(lb), jnp.log1p(-lb) + jax.nn.log_sigmoid(f.astype(jnp.float32)))
    k = -jnp.expm1(log_f)
    heads = lambda t, dim: t.reshape(B, S, HGRN_HEADS, dim)
    o = hgrn2_chunk_scan(heads(q, HGRN_EXPAND), heads(k, HGRN_EXPAND),
                         heads(i.astype(jnp.float32), HGRN_HEAD_V), heads(log_f, HGRN_EXPAND))
    o = rms_norm(o, norm_gain.reshape(HGRN_HEADS, HGRN_HEAD_V)) * \
        jax.nn.silu(heads(g.astype(jnp.float32), HGRN_HEAD_V))
    return o.reshape(B, S, HGRN_VALUE_DIM).astype(h.dtype) @ w_out

def conv_ffn(h, w_up, conv_w, conv_b, w_down):
    u = causal_depthwise_conv(h @ w_up, conv_w, conv_b)
    gate, up = jnp.split(u, 2, axis=-1)
    return (jax.nn.silu(gate) * up) @ w_down

def first_inputs(seed: int = 0) -> dict:
    key = jax.random.key(seed)
    ks = iter(jax.random.split(key, 32))
    D = D_MODEL
    F2 = 2 * FFN_HIDDEN

    def nrm(shape, scale):
        return scale * jax.random.normal(next(ks), shape, jnp.float32)

    def gain(shape):
        return 1.0 + nrm(shape, 0.02)

    return {
        "x": nrm((BATCH, SEQ, D), 1.0),
        "mixer_norm": gain((DEPTH, D)),
        "ffn_norm": gain((DEPTH, D)),
        "attn_w_in": nrm((N_ATTN_LAYERS, D, ATTN_IN_WIDTH), D ** -0.5),
        "attn_q_gain": gain((N_ATTN_LAYERS, ATTN_N_GROUPS, ATTN_HEAD_DIM)),
        "attn_k_gain": gain((N_ATTN_LAYERS, ATTN_N_GROUPS, ATTN_HEAD_DIM)),
        "attn_w_out": nrm((N_ATTN_LAYERS, ATTN_GROUP_WIDTH, D), ATTN_GROUP_WIDTH ** -0.5),
        "conv_w_in": nrm((N_CONV_LAYERS, D, 2 * CONV_CHANNELS), D ** -0.5),
        "conv_b_in": nrm((N_CONV_LAYERS, 2 * CONV_CHANNELS), 0.02),
        "conv_dw_w": nrm((N_CONV_LAYERS, CONV_WIDTH, CONV_CHANNELS), CONV_WIDTH ** -0.5),
        "conv_dw_b": nrm((N_CONV_LAYERS, CONV_CHANNELS), 0.02),
        "conv_ln_g": gain((N_CONV_LAYERS, CONV_CHANNELS)),
        "conv_ln_b": nrm((N_CONV_LAYERS, CONV_CHANNELS), 0.02),
        "conv_w_out": nrm((N_CONV_LAYERS, CONV_CHANNELS, D), CONV_CHANNELS ** -0.5),
        "conv_b_out": nrm((N_CONV_LAYERS, D), 0.02),
        "hgrn_w_in": nrm((N_HGRN_LAYERS, D, 2 * HGRN_KEY_DIM + 2 * HGRN_VALUE_DIM), D ** -0.5),
        "hgrn_lb_logits": nrm((DEPTH, HGRN_KEY_DIM), 1.0),
        "hgrn_norm_g": gain((N_HGRN_LAYERS, HGRN_VALUE_DIM)),
        "hgrn_w_out": nrm((N_HGRN_LAYERS, HGRN_VALUE_DIM, D), HGRN_VALUE_DIM ** -0.5),
        "ffn_w_up": nrm((DEPTH, D, F2), D ** -0.5),
        "ffn_conv_w": nrm((DEPTH, FFN_CONV_WIDTH, F2), FFN_CONV_WIDTH ** -0.5),
        "ffn_conv_b": nrm((DEPTH, F2), 0.02),
        "ffn_w_down": nrm((DEPTH, FFN_HIDDEN, D), FFN_HIDDEN ** -0.5),
    }

def first_block(x, mixer_norm, ffn_norm, attn_w_in, attn_q_gain, attn_k_gain, attn_w_out,
              conv_w_in, conv_b_in, conv_dw_w, conv_dw_b, conv_ln_g, conv_ln_b, conv_w_out,
              conv_b_out, hgrn_w_in, hgrn_lb_logits, hgrn_norm_g, hgrn_w_out,
              ffn_w_up, ffn_conv_w, ffn_conv_b, ffn_w_down):
    lb_cum = jnp.cumsum(jax.nn.softmax(hgrn_lb_logits.astype(jnp.float32), axis=0), axis=0)
    lower_bounds = lb_cum - lb_cum[0]
    for layer in range(DEPTH):
        kind = layer % N_MIXERS
        j = layer // N_MIXERS
        h = rms_norm(x, mixer_norm[layer])
        if kind == 0:
            mix = dilated_attention_mixer(h, attn_w_in[j], attn_q_gain[j], attn_k_gain[j],
                                          attn_w_out[j])
        elif kind == 1:
            mix = conformer_conv_mixer(h, conv_w_in[j], conv_b_in[j], conv_dw_w[j], conv_dw_b[j],
                                       conv_ln_g[j], conv_ln_b[j], conv_w_out[j], conv_b_out[j])
        else:
            mix = hgrn2_mixer(h, hgrn_w_in[j], lower_bounds[layer], hgrn_norm_g[j], hgrn_w_out[j])
        x = x + mix
        x = x + conv_ffn(rms_norm(x, ffn_norm[layer]), ffn_w_up[layer], ffn_conv_w[layer],
                         ffn_conv_b[layer], ffn_w_down[layer])
    return x


MEM_LEN = 256
BLOCK = 128
WINDOW = 128
DA_HEADS = 8
DA_HEAD_DIM = 64
DA_V_DIM = 2 * DA_HEAD_DIM
WA_HEADS = 16
WA_KV_HEADS = 4
WA_HEAD_DIM = 64
XA_HEADS = 4
XA_HEAD_DIM = 256
N_BRANCH = 3
DA_QK_W = DA_HEADS * 2 * DA_HEAD_DIM
DA_V_W = DA_HEADS * DA_V_DIM
WA_Q_W = WA_HEADS * WA_HEAD_DIM
WA_KV_W = WA_KV_HEADS * WA_HEAD_DIM
XA_W = XA_HEADS * XA_HEAD_DIM
GATE_W = N_BRANCH * D_MODEL
IN_WIDTHS = (DA_QK_W, DA_QK_W, DA_V_W, WA_Q_W, WA_KV_W, WA_KV_W, XA_W, GATE_W)
IN_W = sum(IN_WIDTHS)
N_EXPERTS = 16
EC_FACTOR = 2
D_EXPERT = 2048
LAMBDA_STD = 0.1


def rmsnorm(x, g):
    xf = x.astype(jnp.float32)
    y = xf * lax.rsqrt(jnp.mean(xf * xf, axis=-1, keepdims=True) + EPS)
    return (y * g.astype(jnp.float32)).astype(x.dtype)

def alibi_slopes(n_heads):
    return jnp.exp2(-8.0 * jnp.arange(1, n_heads + 1, dtype=jnp.float32) / n_heads)

def lambda_init(layer):
    return 0.8 - 0.6 * float(np.exp(-0.3 * layer))

def diff_attention(q, k, v, lam, subln_g, lam_init):
    b, s = q.shape[0], q.shape[1]
    nb = s // BLOCK
    scale = DA_HEAD_DIM ** -0.5
    slopes = alibi_slopes(DA_HEADS)[None, :, None, None, None]
    kpos = jnp.arange(s)
    qb = jnp.moveaxis(q.reshape(b, nb, BLOCK, DA_HEADS, 2, DA_HEAD_DIM), 1, 0)

    def one_block(args):
        qi, i = args
        sc = jnp.einsum('bqhmd,bkhmd->bhmqk', qi, k).astype(jnp.float32) * scale
        qpos = i * BLOCK + jnp.arange(BLOCK)
        dist = jnp.abs(qpos[:, None] - kpos[None, :]).astype(jnp.float32)
        p = jax.nn.softmax(sc - slopes * dist, axis=-1)
        a = p[:, :, 0] - lam * p[:, :, 1]
        return jnp.einsum('bhqk,bkhe->bqhe', a.astype(v.dtype), v)

    o = lax.map(one_block, (qb, jnp.arange(nb)))
    o = jnp.moveaxis(o, 0, 1).reshape(b, s, DA_HEADS, DA_V_DIM)
    o = rmsnorm(o, subln_g) * (1.0 - lam_init)
    return o.reshape(b, s, DA_V_W)

def window_attention(q, k, v, sink):
    b, s = q.shape[0], q.shape[1]
    nb = s // BLOCK
    span = BLOCK + 2 * WINDOW
    groups = WA_HEADS // WA_KV_HEADS
    scale = WA_HEAD_DIM ** -0.5
    slopes = alibi_slopes(WA_HEADS).reshape(WA_KV_HEADS, groups)[None, :, :, None, None]
    sink_logit = sink.astype(jnp.float32).reshape(WA_KV_HEADS, groups)[None, :, :, None, None]
    pad = ((0, 0), (WINDOW, WINDOW), (0, 0), (0, 0))
    kp = jnp.pad(k, pad)
    vp = jnp.pad(v, pad)
    qb = jnp.moveaxis(q.reshape(b, nb, BLOCK, WA_KV_HEADS, groups, WA_HEAD_DIM), 1, 0)

    def one_block(args):
        qi, i = args
        start = i * BLOCK
        kb = lax.dynamic_slice_in_dim(kp, start, span, axis=1)
        vb = lax.dynamic_slice_in_dim(vp, start, span, axis=1)
        sc = jnp.einsum('bqhgd,bkhd->bhgqk', qi, kb).astype(jnp.float32) * scale
        qpos = start + jnp.arange(BLOCK)
        kpos = start - WINDOW + jnp.arange(span)
        dist = jnp.abs(qpos[:, None] - kpos[None, :])
        valid = (dist <= WINDOW) & ((kpos >= 0) & (kpos < s))[None, :]
        sc = jnp.where(valid, sc - slopes * dist.astype(jnp.float32), -jnp.inf)
        sinks = jnp.broadcast_to(sink_logit, sc.shape[:-1] + (1,))
        p = jax.nn.softmax(jnp.concatenate([sc, sinks], axis=-1), axis=-1)[..., :span]
        return jnp.einsum('bhgqk,bkhd->bqhgd', p.astype(vb.dtype), vb)

    o = lax.map(one_block, (qb, jnp.arange(nb)))
    return jnp.moveaxis(o, 0, 1).reshape(b, s, WA_Q_W)

def memory_attention(q, mk, mv):
    sc = jnp.einsum('bqhd,bkhd->bhqk', q, mk).astype(jnp.float32) * (XA_HEAD_DIM ** -0.5)
    p = jax.nn.softmax(sc, axis=-1)
    o = jnp.einsum('bhqk,bkhd->bqhd', p.astype(mv.dtype), mv)
    return o.reshape(o.shape[0], o.shape[1], XA_W)

def expert_choice_ffn(h, w_router, w_gate, w_up, w_down):
    b, s, _ = h.shape
    cap = max(1, EC_FACTOR * s // N_EXPERTS)
    logits = jnp.einsum('bsd,de->bse', h, w_router).astype(jnp.float32)
    aff = jax.nn.softmax(logits, axis=-1)
    g, idx = lax.top_k(jnp.swapaxes(aff, 1, 2), cap)
    bidx = jnp.arange(b)[:, None, None]
    xe = h[bidx, idx]
    a = jnp.einsum('becd,edf->becf', xe, w_gate)
    u = jnp.einsum('becd,edf->becf', xe, w_up)
    ye = jnp.einsum('becf,efd->becd', jax.nn.silu(a) * u, w_down)
    ye = ye * g[..., None].astype(ye.dtype)
    return jnp.zeros_like(h).at[bidx, idx].add(ye)

def hybrid_layer(x, mem, layer, attn_norm_g, mem_norm_g, w_in, w_mem_kv,
                 da_lambda_q1, da_lambda_k1, da_lambda_q2, da_lambda_k2, da_subln_g,
                 wa_sink, w_da_o, w_wa_o, w_xa_o, w_out, ffn_norm_g,
                 w_router, w_exp_gate, w_exp_up, w_exp_down):
    b, s, d = x.shape
    h = rmsnorm(x, attn_norm_g)
    m = rmsnorm(mem, mem_norm_g)
    proj = h @ w_in
    offsets = np.cumsum(IN_WIDTHS)[:-1].tolist()
    da_q, da_k, da_v, wa_q, wa_k, wa_v, xa_q, gates = jnp.split(proj, offsets, axis=-1)

    lam_init = lambda_init(layer)
    lam = (jnp.exp(jnp.sum(da_lambda_q1.astype(jnp.float32) * da_lambda_k1.astype(jnp.float32)))
           - jnp.exp(jnp.sum(da_lambda_q2.astype(jnp.float32) * da_lambda_k2.astype(jnp.float32)))
           + lam_init)
    o_da = diff_attention(da_q.reshape(b, s, DA_HEADS, 2, DA_HEAD_DIM),
                          da_k.reshape(b, s, DA_HEADS, 2, DA_HEAD_DIM),
                          da_v.reshape(b, s, DA_HEADS, DA_V_DIM),
                          lam, da_subln_g, lam_init)

    o_wa = window_attention(wa_q.reshape(b, s, WA_HEADS, WA_HEAD_DIM),
                            wa_k.reshape(b, s, WA_KV_HEADS, WA_HEAD_DIM),
                            wa_v.reshape(b, s, WA_KV_HEADS, WA_HEAD_DIM),
                            wa_sink)

    mk, mv = jnp.split(m @ w_mem_kv, 2, axis=-1)
    n_mem = mem.shape[1]
    o_xa = memory_attention(xa_q.reshape(b, s, XA_HEADS, XA_HEAD_DIM),
                            mk.reshape(b, n_mem, XA_HEADS, XA_HEAD_DIM),
                            mv.reshape(b, n_mem, XA_HEADS, XA_HEAD_DIM))

    gate = jax.nn.sigmoid(gates.reshape(b, s, N_BRANCH, d))
    merged = (gate[:, :, 0] * (o_da @ w_da_o)
              + gate[:, :, 1] * (o_wa @ w_wa_o)
              + gate[:, :, 2] * (o_xa @ w_xa_o))
    x = x + merged @ w_out

    h2 = rmsnorm(x, ffn_norm_g)
    return x + expert_choice_ffn(h2, w_router, w_exp_gate, w_exp_up, w_exp_down)

def second_inputs(seed: int = 0) -> dict:
    key = jax.random.key(seed)
    ks = jax.random.split(key, 24)
    L, D = DEPTH, D_MODEL

    def w(k, shape, fan_in):
        return jax.random.normal(k, shape, jnp.float32) * (fan_in ** -0.5)

    def gain(k, shape):
        return 1.0 + 0.05 * jax.random.normal(k, shape, jnp.float32)

    def small(k, shape, scale):
        return scale * jax.random.normal(k, shape, jnp.float32)

    return {
        'x': jax.random.normal(ks[0], (BATCH, SEQ, D), jnp.float32),
        'mem': jax.random.normal(ks[1], (BATCH, MEM_LEN, D), jnp.float32),
        'attn_norm_g': gain(ks[2], (L, D)),
        'mem_norm_g': gain(ks[3], (L, D)),
        'w_in': w(ks[4], (L, D, IN_W), D),
        'w_mem_kv': w(ks[5], (L, D, 2 * XA_W), D),
        'da_lambda_q1': small(ks[6], (L, DA_HEAD_DIM), LAMBDA_STD),
        'da_lambda_k1': small(ks[7], (L, DA_HEAD_DIM), LAMBDA_STD),
        'da_lambda_q2': small(ks[8], (L, DA_HEAD_DIM), LAMBDA_STD),
        'da_lambda_k2': small(ks[9], (L, DA_HEAD_DIM), LAMBDA_STD),
        'da_subln_g': gain(ks[10], (L, DA_V_DIM)),
        'wa_sink': small(ks[11], (L, WA_HEADS), 0.5),
        'w_da_o': w(ks[12], (L, DA_V_W, D), DA_V_W),
        'w_wa_o': w(ks[13], (L, WA_Q_W, D), WA_Q_W),
        'w_xa_o': w(ks[14], (L, XA_W, D), XA_W),
        'w_out': w(ks[15], (L, D, D), D),
        'ffn_norm_g': gain(ks[16], (L, D)),
        'w_router': w(ks[17], (L, D, N_EXPERTS), D),
        'w_exp_gate': w(ks[18], (L, N_EXPERTS, D, D_EXPERT), D),
        'w_exp_up': w(ks[19], (L, N_EXPERTS, D, D_EXPERT), D),
        'w_exp_down': w(ks[20], (L, N_EXPERTS, D_EXPERT, D), D_EXPERT),
        'final_norm_g': gain(ks[21], (D,)),
    }

def second_block(x, mem, attn_norm_g, mem_norm_g, w_in, w_mem_kv,
              da_lambda_q1, da_lambda_k1, da_lambda_q2, da_lambda_k2, da_subln_g,
              wa_sink, w_da_o, w_wa_o, w_xa_o, w_out, ffn_norm_g,
              w_router, w_exp_gate, w_exp_up, w_exp_down, final_norm_g):
    for l in range(DEPTH):
        x = hybrid_layer(x, mem, l, attn_norm_g[l], mem_norm_g[l], w_in[l], w_mem_kv[l],
                         da_lambda_q1[l], da_lambda_k1[l], da_lambda_q2[l], da_lambda_k2[l],
                         da_subln_g[l], wa_sink[l], w_da_o[l], w_wa_o[l], w_xa_o[l], w_out[l],
                         ffn_norm_g[l], w_router[l], w_exp_gate[l], w_exp_up[l], w_exp_down[l])
    return rmsnorm(x, final_norm_g)


def setup_inputs(seed=0):
    out = dict(first_inputs(seed))
    for name, value in second_inputs(seed + 1).items():
        if name != "x":
            out[name + "_2"] = value
    return out


def reference(
    x, mixer_norm, ffn_norm, attn_w_in, attn_q_gain, attn_k_gain, attn_w_out, conv_w_in,
    conv_b_in, conv_dw_w, conv_dw_b, conv_ln_g, conv_ln_b, conv_w_out, conv_b_out, hgrn_w_in,
    hgrn_lb_logits, hgrn_norm_g, hgrn_w_out, ffn_w_up, ffn_conv_w, ffn_conv_b, ffn_w_down,
    mem_2, attn_norm_g_2, mem_norm_g_2, w_in_2, w_mem_kv_2, da_lambda_q1_2, da_lambda_k1_2,
    da_lambda_q2_2, da_lambda_k2_2, da_subln_g_2, wa_sink_2, w_da_o_2, w_wa_o_2, w_xa_o_2,
    w_out_2, ffn_norm_g_2, w_router_2, w_exp_gate_2, w_exp_up_2, w_exp_down_2, final_norm_g_2,
):
    x = first_block(
        x, mixer_norm, ffn_norm, attn_w_in, attn_q_gain, attn_k_gain, attn_w_out, conv_w_in,
        conv_b_in, conv_dw_w, conv_dw_b, conv_ln_g, conv_ln_b, conv_w_out, conv_b_out,
        hgrn_w_in, hgrn_lb_logits, hgrn_norm_g, hgrn_w_out, ffn_w_up, ffn_conv_w, ffn_conv_b,
        ffn_w_down,
    )
    return second_block(
        x, mem_2, attn_norm_g_2, mem_norm_g_2, w_in_2, w_mem_kv_2, da_lambda_q1_2,
        da_lambda_k1_2, da_lambda_q2_2, da_lambda_k2_2, da_subln_g_2, wa_sink_2, w_da_o_2,
        w_wa_o_2, w_xa_o_2, w_out_2, ffn_norm_g_2, w_router_2, w_exp_gate_2, w_exp_up_2,
        w_exp_down_2, final_norm_g_2,
    )


_drawn_inputs = setup_inputs


def setup_inputs(seed=0):
    import zlib

    import numpy as np

    out = dict(_drawn_inputs(seed))
    spreads = {}
    factors = {'mixer_norm': 5.975,
     'ffn_norm': 2.765,
     'attn_q_gain': 8.0,
     'attn_k_gain': 8.0,
     'mem_norm_g_2': 8.0,
     'da_lambda_q1_2': 2.908,
     'da_subln_g_2': 21.504,
     'wa_sink_2': 64.0,
     'ffn_conv_b': 5.329,
     'da_lambda_k2_2': 5.722,
     'w_wa_o_2': 5.561,
     'ffn_norm_g_2': 8.0,
     'w_router_2': 2.784,
     'w_exp_gate_2': 2.791}
    for name, (base, spread) in spreads.items():
        noise = np.random.default_rng([zlib.crc32(name.encode()), seed]).standard_normal(out[name].shape)
        drawn = base * np.exp(spread * noise) if base else spread * noise
        out[name] = __import__('jax').numpy.asarray(drawn.astype(out[name].dtype))
    for name, factor in factors.items():
        out[name] = (out[name] * factor).astype(out[name].dtype)
    return out
```

```python
import concourse.bass as bass
from concourse import mybir
from contextlib import ExitStack

S, D, P = 512, 1024, 128
TT, KT = S // P, D // P
EPS = 1e-6
NEG = -1e30
GROUPS, HEADS1, DH = 3, 8, 64
GW = HEADS1 * DH
FH, FB = 2816, 2816 // P
MEM = 256
DA_H, WA_H, WA_KV, XA_H, NB = 8, 16, 4, 4, 3
NE, CAP, FE = 16, 64, 2048
PAIRS, FT = NE // 2, FE // P
NS, SLOT = 8, 2048
COL = {}
_at = 0
for _n, _w in (("daq", 1024), ("dak", 1024), ("dav", 1024), ("waq", 1024), ("wak", 256),
               ("wav", 256), ("xaq", 1024), ("gate", 3072)):
    COL[_n] = _at
    _at += _w
MIXG, FFNG, ATTG, MEMG, FFN2G, CB, CW = 0, 8, 16, 24, 32, 40, 84
QG, KG, SUBG, NVEC = 216, 219, 222, 223
NORM_TILES = [TT, TT, TT, MEM // P, TT]
WA_KB = [[0, 1], [0, 1, 2], [1, 2, 3], [2, 3]]
WA_BLOCKS = [(qb, kb) for qb in range(4) for kb in WA_KB[qb]]


def build(nc, I, out):
    f32, i32 = mybir.dt.float32, mybir.dt.int32
    ALU, ACT, AX = mybir.AluOpType, mybir.ActivationFunctionType, mybir.AxisListType
    ctx = ExitStack()
    with ctx:
        def sb(name, shape, dt=f32):
            return ctx.enter_context(nc.sbuf_tensor(name, shape, dt))

        def sem(name):
            return ctx.enter_context(nc.semaphore(name))

        ring = sb("ring", [P, NS, SLOT])
        x = sb("x", [P, TT, D])
        hT = sb("hT", [P, KT, S])
        arena = sb("arena", [P, 27264])
        ident = sb("ident", [P, P])
        mean64 = sb("mean64", [P, P])
        mean128 = sb("mean128", [P, P])
        vec = sb("vec", [P, NVEC])
        wr = sb("wr", [P, KT, NE])
        epsb = sb("epsb", [P, 1])
        ssq = sb("ssq", [P, TT])
        rstd = sb("rstd", [P, TT])
        nm1 = sb("nm1", [P, GROUPS, TT, HEADS1])
        l1 = sb("l1", [P, GROUPS, TT, HEADS1])
        sink = sb("sink", [P, WA_H])
        lamsc = sb("lamsc", [P, 4])
        mx = sb("mx", [P, 2, 4])
        nmx = sb("nmx", [P, 2, 4])
        lsum = sb("lsum", [P, 2, 4])
        esink = sb("esink", [P, 2, 4])
        rl = sb("rl", [P, 2, 4])
        ps = ctx.enter_context(nc.psum_tensor("ps", [P, 8, 512], f32))

        def ar(off, *shape):
            n = 1
            for s in shape:
                n *= s
            v = arena[:, off:off + n]
            if len(shape) == 2:
                v = v.rearrange("p (a b) -> p a b", a=shape[0])
            elif len(shape) == 3:
                v = v.rearrange("p (a b c) -> p a b c", a=shape[0], b=shape[1])
            return v

        qk = ar(0, 8, S)
        v1 = ar(4096, TT, GW)
        U = ar(6144, GROUPS, 4, S)
        mask = ar(12288, 4, 512)
        sm = ar(14336, 3, 512)
        pt1 = ar(15872, 2, 512)
        sq = ar(16896, 2, 512)
        rt = ar(17920, 2, 512)
        rr = ar(18944, 2, 512)
        rows = ar(19968, 6, 512)[0:HEADS1]
        oT = ar(23040, 4, S)
        selB = ar(25088, 4, P)[0:HEADS1]
        m2i = arena[:, 25600:26112].bitcast(i32)
        coef = ar(14336, 3, 512)[0:HEADS1]
        crow = ar(15872, 2, 512)[0:HEADS1]
        ctmp = ar(16896, 2, 512)
        vrow = ar(0, 4, P)
        xn = ar(19968, TT, D)
        junk = ar(24064, D)
        actT = ar(0, FB, S)
        cg = ar(11264, 2, S)
        cu = ar(12288, 2, S)
        o_da, o_wa, o_xa = ar(0, KT, S), ar(4096, KT, S), ar(8192, KT, S)
        da_q, da_k, da_v = ar(12288, KT, S), ar(16384, KT, S), ar(20480, TT, D)
        da_e = ar(4096, 2, 4, S)
        da_pt = ar(8192, 8, S)
        dist = ar(24576, 896)
        alibi = ar(25472, 2, 896)
        lamv = ar(8192, 4, 64)
        wa_q, wa_k, wa_v = ar(12288, KT, S), ar(16384, WA_KV, S), ar(18432, TT, 256)
        wa_p = ar(19456, 2, 4, 384)
        wa_pt = ar(22528, 20, P)
        wdist = ar(25600, 384)
        walibi = ar(25984, 2, 384)
        memt = ar(8192, 2, D)
        memn = ar(10240, 2, D)
        memT = ar(16384, KT, MEM)
        xa_q, mkT, mv = ar(12288, KT, S), ar(18432, KT, MEM), ar(20480, 2, D)
        xa_p = ar(22528, 2, 4, MEM)
        xa_pt = ar(24576, 4, S)
        merged = ar(12288, KT, S)
        sg = ar(16384, 2, S)
        gtmp = ar(17408, 2, S)
        h2 = ar(0, TT, D)
        OH = ar(4096, TT, NE * CAP)
        ohgT = ar(8192, PAIRS, S)
        xeT = ar(12288, KT, P)
        act_e = ar(13312, FT, CAP)
        Y = ar(14336, D)
        ohst = ar(15360, S)
        act_tok = ar(19968, FE // 2)
        sg_e = ar(22016, FE)
        h2g = ar(16896, D)
        fing = ar(17920, D)
        iota1 = ar(18944, CAP)
        aff = ar(19008, TT, NE)
        lg = ar(19072, TT, NE)
        slotT = ar(19136, TT, NE)
        small = ar(19200, 16)
        top = ar(19216, CAP)[0:NE]
        xn2 = ar(19968, TT, D)
        OHg = ar(19968, TT, NE * CAP)
        affT = ar(24096, S)[0:NE]
        wk = ar(24608, S)[0:NE]
        gt = ar(25120, S)[0:NE]
        eq = ar(25632, S)[0:NE]
        cum = ar(26144, S)[0:NE]
        ones = ar(26656, S)[0:NE]

        landed = [sem(f"landed{i}") for i in range(NS)]
        dn_w, e_chunks, slots_ready, tr_ps = sem("dn_w"), sem("e_chunks"), sem("slots_ready"), sem("tr_ps")
        in_x, in_vec, in_small, in_moe, in_mem = sem("in_x"), sem("in_vec"), sem("in_small"), sem("in_moe"), sem("in_mem")
        pool_c, act_c, dve_c = sem("pool_chain"), sem("act_chain"), sem("dve_chain")
        consts, masks_done, m2i_ready, m2_ready = sem("consts"), sem("masks_done"), sem("m2i_ready"), sem("m2_ready")
        vec_ps, vec_done = sem("vec_ps"), sem("vec_done")
        n_sq, n_rt, n_xn, n_tp, n_evA, n_evD = (sem(n) for n in ("n_sq", "n_rt", "n_xn", "n_tp", "n_evA", "n_evD"))
        qk_ps, sq_done, ssq_ps, rt_done, rr_done, qk_done = (sem(n) for n in ("qk_ps", "sq_done", "ssq_ps", "rt_done", "rr_done", "qk_done"))
        v_ps, v_ev = sem("v_ps"), sem("v_ev")
        s_ps, sm_done, nm_done, p_done, t_ps, pt_done, pv_done, o_ev = (sem(n) for n in ("s_ps", "sm_done", "nm_done", "p_done", "t_ps", "pt_done", "pv_done", "o_ev"))
        r_ps, rowd, rowexp, coef_done, bc_ps, bc_done = (sem(n) for n in ("r_ps", "rowd", "rowexp", "coef_done", "bc_ps", "bc_done"))
        wo_ps, x1_done = sem("wo_ps"), sem("x1_done")
        f_ps, f_id, conv_done, silu_done, act_done = (sem(n) for n in ("f_ps", "f_id", "conv_done", "silu_done", "act_done"))
        dn_ps, x2_done = sem("dn_ps"), sem("x2_done")
        pj_ps, pjA, pjD = sem("pj_ps"), sem("pjA"), sem("pjD")
        dist_done, al_done, wal_done = sem("dist_done"), sem("al_done"), sem("wal_done")
        sd_ps, sd_done, dnm_done, de_done, a_done, dt_ps, dpt_done, dpv, dO_ev = (sem(n) for n in ("sd_ps", "sd_done", "dnm_done", "de_done", "a_done", "dt_ps", "dpt_done", "dpv", "dO_ev"))
        lam_sum, lam_exp, lam_done = sem("lam_sum"), sem("lam_exp"), sem("lam_done")
        on_sq, on_ps, on_rt, on_rr, on_done = (sem(n) for n in ("on_sq", "on_ps", "on_rt", "on_rr", "on_done"))
        sw_ps, sw_done, wnm_done, we_done, aw_done, wt_ps, wpt_done, wpv, wO_ev = (sem(n) for n in ("sw_ps", "sw_done", "wnm_done", "we_done", "aw_done", "wt_ps", "wpt_done", "wpv", "wO_ev"))
        sx_ps, xnm_done, xe1_done, ax_done, xt_ps, xpt_done, xpv, xO_ev = (sem(n) for n in ("sx_ps", "xnm_done", "xe1_done", "ax_done", "xt_ps", "xpt_done", "xpv", "xO_ev"))
        g_ps, gsig, m_done = sem("gate_ps"), sem("gate_sig"), sem("m_done")
        wo2_ps, x3_done = sem("wo2_ps"), sem("x3_done")
        h2_done, rt_ps, lg_done, lexp, affd, affT_ps, slot_d, slot_ps, oh_done, ohg_done, og_ps, og_ev = (sem(n) for n in ("h2_done", "rt_ps", "lg_done", "lexp", "affd", "affT_ps", "slot_d", "slot_ps", "oh_done", "ohg_done", "og_ps", "og_ev"))
        ga_ps, b67_free, sg_done, ae_done, ye_done, st_done, c_ps = (sem(n) for n in ("ga_ps", "b67_free", "sg_done", "ae_done", "ye_done", "st_done", "c_ps"))
        f_sq, f_rt, o_done, out_done = sem("f_sq"), sem("f_rt"), sem("o_done"), sem("out_done")

        PJ = "A" * 8 + "D" * 8 + "ADAD" * 2
        PJ_WA = len(PJ)
        PJ += "A" * 8 + "DD" + "ADAD"
        PJ_XA = len(PJ)
        PJ += "D" * 8 + "DDDD" + "A" * 8

        def pj_bank_free(eng, n):
            if n >= 4:
                m = n - 4
                eng.wait_ge(pjA if PJ[m] == "A" else pjD, PJ[:m + 1].count(PJ[m]))

        def pj_all_done(eng, n):
            eng.wait_ge(pjA, PJ[:n].count("A"))
            eng.wait_ge(pjD, PJ[:n].count("D"))

        def cols_all_k(w, c0, n):
            return w[:, c0:c0 + n].rearrange("(k p) n -> p k n", p=P)

        def rows_k(w, k0, nk, c0, n):
            return w[k0 * P:(k0 + nk) * P, c0:c0 + n].rearrange("(k p) n -> p k n", p=P)

        def col_chunks(w, c0, n):
            return [cols_all_k(w, c, 256) for c in range(c0, c0 + n, 256)]

        def tok_chunks(w, c0, n, nk=KT):
            return [rows_k(w, k, 4, c, 512) for c in range(c0, c0 + n, 512) for k in range(0, nk, 4)]

        chunks = []

        def chunk(srcs, done, value, step):
            for i, src in enumerate(srcs):
                chunks.append((src, done, value + (i + 1) * step))

        w1, wi, wm = I["attn_w_in"][0], I["w_in_2"][0], I["w_mem_kv_2"][0]
        for g in range(GROUPS):
            b = 3 * g * GW
            chunk(col_chunks(w1, b, 2 * GW), qk_ps, 8 * g, 2)
            chunk(tok_chunks(w1, b + 2 * GW, GW), v_ps, TT * (g + 1), 0)
        chunk(tok_chunks(I["attn_w_out"][0], 0, D, GW // P), wo_ps, 0, 4)
        for jj in range(FB // 2):
            for c in (0, FH):
                chunk(col_chunks(I["ffn_w_up"][0], c + 256 * jj, 256), f_ps, 4 * (jj + 1), 0)
        for f in range(0, FB, 2):
            last = f == FB - 2
            chunk([rows_k(I["ffn_w_down"][0], f, 2, 0, D)], dn_ps if last else dn_w, 8 if last else f // 2 + 1, 0)
        chunk(col_chunks(wi, COL["daq"], 2048), pj_ps, 0, 2)
        for half in range(2):
            chunk(tok_chunks(wi, COL["dav"] + 512 * half, 512), pj_ps, 20 + 4 * half, 0)
        chunk(col_chunks(wi, COL["waq"], 1280), pj_ps, PJ_WA, 2)
        chunk(col_chunks(wi, COL["wav"], 256), pj_ps, PJ_WA + 14, 0)
        chunk(col_chunks(wm, 0, D), pj_ps, PJ_XA, 2)
        for half in range(2):
            chunk(tok_chunks(wm, D + 512 * half, 512), pj_ps, PJ_XA + 10 + 2 * half, 0)
        chunk(col_chunks(wi, COL["xaq"], 1024), pj_ps, PJ_XA + 12, 2)
        wb = [I["w_da_o_2"][0], I["w_wa_o_2"][0], I["w_xa_o_2"][0]]
        for jj in range(4):
            for b in range(NB):
                n = 4 * (jj * NB + b + 1)
                chunk(col_chunks(wi, COL["gate"] + b * D + jj * 256, 256), g_ps, n, 0)
                chunk(col_chunks(wb[b], jj * 256, 256), g_ps, n, 0)
        for half in range(2):
            chunk(tok_chunks(I["w_out_2"][0], 512 * half, 512), wo2_ps, 4 * (half + 1), 0)
        NCH = len(chunks)
        SEQ = 14
        ECH = 48
        wg_e, wu_e, wd_e = (I[n].rearrange("l e a b -> (l e a b)")
                            for n in ("w_exp_gate_2", "w_exp_up_2", "w_exp_down_2"))

        units = []
        for g in range(GROUPS):
            for h in range(HEADS1):
                units += [(g, h, [0, 1]), (g, h, [2, 3])] if g == 0 else [(g, h, [0, 1, 2, 3])]
        UB = [0, 16, 24, 32]
        head_end = {}
        for n, (g, h, _) in enumerate(units):
            head_end[(g, h)] = n + 1
        nbase = [sum(NORM_TILES[:k]) for k in range(6)]

        block = ctx.enter_context(nc.Block())

        @block.sync
        def _(sp):
            for c, (src, _, _) in enumerate(chunks):
                if c >= NS:
                    _, done, value = chunks[c - NS]
                    sp.wait_ge(done, value)
                dst = ring[:, c % NS, :].rearrange("p (k n) -> p k n", k=src.shape[1])
                sp.dma_start(dst, src).then_inc(landed[c % NS], 16)

            def expert_chunk(at, c, free=None):
                a, i = c // 24, c % 24
                s = (NCH + c) % NS
                if i < 16:
                    w, k, dst = (wg_e, wu_e)[i % 2], i // 2, ring[:, s, :]
                else:
                    w, k, dst = wd_e, i - 16, ring[:, s, :].rearrange("p (j n) -> p j n", j=2)
                at = at + (8 * a + k) * P * SLOT
                if free is not None:
                    sp.wait_ge(e_chunks, free)
                src = w[bass.ds(at, P * SLOT)]
                if i < 16:
                    src = src.rearrange("(p n) -> p n", p=P)
                else:
                    src = src.rearrange("(j p n) -> p j n", p=P, j=2)
                sp.dma_start(dst, src).then_inc(landed[s], 16)

            PAIR_W = 2 * D * FE
            for c in range(NS):
                _, done, value = chunks[NCH - NS + c]
                sp.wait_ge(done, value)
                expert_chunk(0, c)
            with sp.Fori(0, PAIRS - 1) as q:
                for c in range(ECH):
                    n = c + NS
                    free = None if n == 16 else q * ECH + (c + (2 if n == 15 else 1))
                    expert_chunk(q * PAIR_W + n // ECH * PAIR_W, n % ECH, free)
            for c in range(ECH - NS):
                sp.wait_ge(e_chunks, (PAIRS - 1) * ECH + c + 1)
                expert_chunk((PAIRS - 1) * PAIR_W, c + NS)
            for t in range(TT):
                sp.wait_ge(o_done, t + 1)
                sp.dma_start(out[0, t * P:(t + 1) * P, :], xn2[:, t, :]).then_inc(out_done, 16)
            sp.wait_ge(out_done, 16 * TT)

        @block.gpsimd
        def _(pool):
            n = [0]

            def link(ins):
                n[0] += 1
                ins.then_inc(pool_c, 1)
                pool.wait_ge(pool_c, n[0])

            nc.gpsimd.memset(ident[:], 0.0)
            nc.gpsimd.memset(mean64[:], 0.0)
            nc.gpsimd.memset(epsb[:], EPS)
            nc.gpsimd.memset(mean128[:], 1.0 / 128)
            link(nc.gpsimd.memset(mask[:], 0.0))
            nc.gpsimd.memset(selB[:], 0.0)
            nc.gpsimd.memset(mean64[0:64, 0:64], 1.0 / 64)
            link(nc.gpsimd.memset(mean64[64:128, 64:128], 1.0 / 64))
            nc.gpsimd.affine_select(out=ident[:], in_=ident[:], compare_op=ALU.not_equal, fill=1.0, base=0,
                                    pattern=[[-1, P]], channel_multiplier=1).then_inc(consts, 1)
            nc.gpsimd.iota(m2i.rearrange("p (c k) -> p c k", c=4), pattern=[[0, 4], [-1, P]], base=P,
                           channel_multiplier=1).then_inc(m2i_ready, 1)
            s4 = selB.rearrange("p b (a c) -> p b a c", a=2)
            nc.gpsimd.affine_select(out=s4, in_=s4, compare_op=ALU.not_equal, fill=1.0, base=0,
                                    pattern=[[-2, 4], [-1, 2], [0, 64]], channel_multiplier=1)

            def causal(v, nt):
                return nc.gpsimd.affine_select(out=v, in_=v, compare_op=ALU.is_ge, fill=NEG, base=0,
                                               pattern=[[0, nt], [-1, P]], channel_multiplier=1)

            m0 = mask[:, 0:2, :].rearrange("p a (t s k) -> p (a t) s k", t=2, s=2)
            causal(m0[:, :, 1, :], 4)
            pv = m0[:, :, 0, :]
            link(nc.gpsimd.affine_select(out=pv, in_=pv, compare_op=ALU.is_ge, fill=NEG, base=0,
                                         pattern=[[0, 4], [1, P]], channel_multiplier=-1))
            nc.gpsimd.memset(m0[:, 0, 0, :], NEG)
            causal(mask[:, 2, :].rearrange("p (c k) -> p c k", c=4), 4)
            pool.wait_ge(m2_ready, 1)
            causal(mask[:, 3, :].rearrange("p (c k) -> p c k", c=4), 4).then_inc(masks_done, 1)

            pool.wait_ge(x2_done, 8)
            pool.wait_ge(n_xn, nbase[3])
            link(nc.gpsimd.iota(dist, pattern=[[-1, 896]], base=384, channel_multiplier=1,
                                allow_small_or_imprecise_dtypes=True))
            link(nc.gpsimd.tensor_scalar(alibi[:, 0, :], dist, 0.0, 2.0, ALU.max, ALU.mult))
            link(nc.gpsimd.tensor_tensor(dist, alibi[:, 0, :], dist, ALU.subtract))
            for h in range(DA_H):
                if h >= 2:
                    pool.wait_ge(sd_done, 8 * (h - 1))
                nc.gpsimd.tensor_scalar(alibi[:, h % 2, :], dist, -(2.0 ** (-8.0 * (h + 1) / DA_H)), None,
                                        ALU.mult).then_inc(al_done, 1)
            pool.wait_ge(sd_done, 64)
            link(nc.gpsimd.iota(wdist, pattern=[[-1, 384]], base=P, channel_multiplier=1,
                                allow_small_or_imprecise_dtypes=True))
            link(nc.gpsimd.tensor_scalar(walibi[:, 0, :], wdist, 0.0, 2.0, ALU.max, ALU.mult))
            link(nc.gpsimd.tensor_tensor(wdist, walibi[:, 0, :], wdist, ALU.subtract))
            link(nc.gpsimd.affine_select(out=wdist, in_=wdist, compare_op=ALU.is_ge, fill=-NEG, base=0,
                                         pattern=[[1, 384]], channel_multiplier=-1))
            link(nc.gpsimd.affine_select(out=wdist, in_=wdist, compare_op=ALU.is_ge, fill=-NEG, base=256,
                                         pattern=[[-1, 384]], channel_multiplier=1))
            for h in range(WA_H):
                if h >= 2:
                    pool.wait_ge(sw_done, 4 * (h - 1))
                nc.gpsimd.tensor_scalar(walibi[:, h % 2, :], wdist, -(2.0 ** (-8.0 * (h + 1) / WA_H)), None,
                                        ALU.mult).then_inc(wal_done, 1)

            pool.wait_ge(x3_done, 8)
            nc.gpsimd.iota(iota1, pattern=[[1, CAP]], base=1, channel_multiplier=0,
                           allow_small_or_imprecise_dtypes=True)
            nc.gpsimd.memset(ones, 1.0).then_inc(slots_ready, 1)
            for t in range(TT):
                pool.wait_ge(oh_done, t + 1)
                nc.gpsimd.tensor_tensor(OHg[:, t, :].rearrange("p (e c) -> p e c", e=NE),
                                        OH[:, t, :].rearrange("p (e c) -> p e c", e=NE),
                                        aff[:, t, :].unsqueeze(2).to_broadcast([P, NE, CAP]),
                                        ALU.mult).then_inc(ohg_done, 1)

        @block.scalar
        def _(act):
            A = nc.scalar.activation
            F = ACT
            act.dma_start(x[:], I["x"][0].rearrange("(t p) d -> p t d", p=P)).then_inc(in_x, 16)
            for i, n in enumerate(("mixer_norm", "ffn_norm", "attn_norm_g_2", "mem_norm_g_2", "ffn_norm_g_2")):
                act.dma_start(vrow[8 * i:8 * i + 8, 0, :],
                              I[n][0].rearrange("(k p) -> k p", p=P)).then_inc(in_vec, 16)
            act.dma_start(vrow[CB:CB + 44, 0, :], I["ffn_conv_b"][0].rearrange("(k p) -> k p", p=P)).then_inc(in_vec, 16)
            act.dma_start(vrow[0:88, 1, :], I["ffn_conv_w"][0, 0:2].rearrange("a (k p) -> (a k) p", p=P)).then_inc(in_vec, 16)
            act.dma_start(vrow[0:44, 2, :], I["ffn_conv_w"][0, 2].rearrange("(k p) -> k p", p=P)).then_inc(in_vec, 16)
            for half in range(2):
                c = slice(64 * half, 64 * half + 64)
                act.dma_start(vrow[0:3, 3, c], I["attn_q_gain"][0]).then_inc(in_vec, 16)
                act.dma_start(vrow[3:6, 3, c], I["attn_k_gain"][0]).then_inc(in_vec, 16)
            act.dma_start(vrow[6:7, 3, :], I["da_subln_g_2"]).then_inc(in_vec, 16)
            act.dma_start(wr[:], I["w_router_2"][0].rearrange("(k p) e -> p k e", p=P)).then_inc(in_small, 16)
            act.dma_start(sink[:], I["wa_sink_2"].partition_broadcast(P).rearrange("p a h -> p (a h)")).then_inc(in_small, 16)

            def norm(k, src, xbuf):
                nt = NORM_TILES[k]
                if k:
                    act.wait_ge(n_xn, nbase[k])
                for t in range(nt):
                    if t:
                        act.wait_ge(n_sq, nbase[k] + t)
                    A(xbuf, src[:, t, :], F.Square, accum_out=ssq[:, t:t + 1]).then_inc(n_sq, 1)
                act.wait_ge(n_sq, nbase[k + 1])
                A(ssq[:, 0:nt], ssq[:, 0:nt], F.Sqrt, bias=epsb[:], scale=1.0 / D).then_inc(n_rt, 1)

            def norm_out(k, dst, gain, ntok):
                for kb in range(0, KT, 2):
                    act.wait_ge(n_tp, 8 * k + kb + 1)
                    A(dst[:, kb, :], ps[:, kb % 4, 0:ntok], F.Copy, scale=vec[:, gain + kb:gain + kb + 1]).then_inc(n_evA, 1)

            act.wait_ge(in_x, 16)
            act.wait_ge(consts, 1)
            norm(0, x, junk)
            act.wait_ge(vec_done, 1)
            norm_out(0, hT, MIXG, S)

            for g in range(GROUPS):
                for b in range(9):
                    n = 8 * g + b
                    if b < 8:
                        act.wait_ge(qk_ps, n + 1)
                        if n >= 2:
                            act.wait_ge(ssq_ps, n - 1)
                        A(sq[:, n % 2, :], ps[:, n % 4, :], F.Square).then_inc(sq_done, 1)
                    if b:
                        m = n - 1
                        act.wait_ge(ssq_ps, m + 1)
                        if m >= 2:
                            act.wait_ge(rr_done, m - 1)
                        A(rt[:, m % 2, :], ps[:, 6 + m % 2, :], F.Sqrt, bias=epsb[:]).then_inc(rt_done, 1)
                for t in range(TT):
                    act.wait_ge(v_ps, TT * g + t + 1)
                    A(v1[:, t, :], ps[:, 4 + t, :], F.Copy).then_inc(v_ev, 1)
                for u in range(UB[g], UB[g + 1] + 2):
                    if u < UB[g + 1]:
                        _, h, tiles = units[u]
                        w = 512 // len(tiles)
                        act.wait_ge(nm_done, u + 1)
                        for i, t in enumerate(tiles):
                            last = A(sm[:, u % 3, i * w:(i + 1) * w], sm[:, u % 3, i * w:(i + 1) * w], F.Exp,
                                     bias=nm1[:, g, t, h:h + 1], accum_out=l1[:, g, t, h:h + 1])
                        last.then_inc(p_done, 1)
                    m = u - 2
                    if m >= UB[g] and head_end[units[m][0:2]] == m + 1:
                        h = units[m][1]
                        act.wait_ge(pv_done, m + 1)
                        r = slice(64 * (h % 2), 64 * (h % 2) + 64)
                        o, i_ = U[r, g, h // 2, :], ps[r, 2 + h % 2, :]
                        if g:
                            o = o.rearrange("p (j c) -> p c j", c=4)
                            i_ = i_.rearrange("p (c j) -> p c j", c=4)
                        A(o, i_, F.Copy).then_inc(o_ev, 1)
            act.wait_ge(rowd, 1)
            A(coef, coef, F.Exp).then_inc(rowexp, 1)

            act.wait_ge(x1_done, 8)
            norm(1, x, junk)
            norm_out(1, hT, FFNG, S)
            for j in range(FB + 1):
                if j < FB:
                    for i, buf in enumerate((cg, cu)):
                        act.wait_ge(f_ps, 2 * j + i + 1)
                        if j >= 2:
                            act.wait_ge(act_done, j - 1)
                        A(buf[:, j % 2, :], ps[:, 2 * (j % 2) + i, :], F.Identity,
                          bias=vec[:, CB + 22 * i + j:CB + 22 * i + j + 1],
                          scale=vec[:, CW + 88 + 22 * i + j:CW + 88 + 22 * i + j + 1]).then_inc(f_id, 1)
                if j:
                    act.wait_ge(conv_done, 4 * (j - 1) + 3)
                    A(cg[:, (j - 1) % 2, :], cg[:, (j - 1) % 2, :], F.Silu).then_inc(silu_done, 1)

            act.wait_ge(x2_done, 8)
            norm(2, x, junk)
            norm_out(2, hT, ATTG, S)
            for i, n in enumerate(("da_lambda_q1_2", "da_lambda_k1_2", "da_lambda_q2_2", "da_lambda_k2_2")):
                act.dma_start(lamv[:, i, :], I[n].partition_broadcast(P).rearrange("p a d -> p (a d)")).then_inc(in_small, 16)
            for n in range(8):
                act.wait_ge(pj_ps, n + 1)
                A(da_q[:, n, :], ps[:, n % 4, :], F.Copy, scale=0.125).then_inc(pjA, 1)
            for n in range(16, 24):
                if PJ[n] == "A":
                    t, half = (n - 16) % 4, (n - 16) // 4
                    act.wait_ge(pj_ps, n + 1)
                    A(da_v[:, t, half * 512:half * 512 + 512], ps[:, n % 4, :], F.Copy).then_inc(pjA, 1)
            act.wait_ge(lam_sum, 1)
            A(lamsc[:, 0:2], lamsc[:, 0:2], F.Exp).then_inc(lam_exp, 1)

            def da_copy(u):
                h = u // 2
                for i in range(2):
                    qb = 2 * (u % 2) + i
                    act.wait_ge(dt_ps, 2 * u + i + 1)
                    if h >= 2:
                        act.wait_ge(dpv, h - 1)
                    A(da_pt[:, 4 * (h % 2):4 * (h % 2) + 4, qb * P:(qb + 1) * P],
                      ps[:, i, :].rearrange("p (k q) -> p k q", k=4), F.Copy).then_inc(dpt_done, 1)

            def da_out(h):
                act.wait_ge(dpv, h + 1)
                A(o_da[:, h, :], ps[:, 2 + h % 2, :], F.Copy).then_inc(dO_ev, 1)

            for u in range(16 + 3):
                if u < 16:
                    act.wait_ge(dnm_done, u + 1)
                    for i in range(4):
                        last = A(da_e[:, u % 2, i, :], da_e[:, u % 2, i, :], F.Exp, bias=nmx[:, u % 2, i:i + 1],
                                 accum_out=lsum[:, u % 2, i:i + 1])
                    last.then_inc(de_done, 1)
                if 1 <= u <= 16:
                    da_copy(u - 1)
                if u >= 4 and u % 2 == 0:
                    da_out(u // 2 - 2)
            act.wait_ge(dpv, 8)
            for h in range(9):
                if h < 8:
                    act.wait_ge(dO_ev, h + 1)
                    if h >= 2:
                        act.wait_ge(on_ps, h - 1)
                    A(da_e[:, 0, h % 2, :], o_da[:, h, :], F.Square).then_inc(on_sq, 1)
                if h:
                    m = h - 1
                    act.wait_ge(on_ps, m + 1)
                    if m >= 2:
                        act.wait_ge(on_rr, m - 1)
                    A(da_e[:, 0, 2 + m % 2, :], ps[:, 4 + m % 2, :], F.Sqrt, bias=epsb[:]).then_inc(on_rt, 1)

            act.dma_start(memt, I["mem_2"][0].rearrange("(t p) d -> p t d", p=P)).then_inc(in_mem, 16)
            for n in range(PJ_WA, PJ_XA):
                if PJ[n] == "A":
                    m = n - PJ_WA
                    act.wait_ge(pj_ps, n + 1)
                    if m < 8:
                        A(wa_q[:, m, :], ps[:, n % 4, :], F.Copy, scale=0.125).then_inc(pjA, 1)
                    else:
                        A(wa_v[:, m - 10, :], ps[:, n % 4, 0:256], F.Copy).then_inc(pjA, 1)

            def wa_copy(h):
                for i, nb in enumerate((4, 4, 2)):
                    m = 3 * h + i
                    act.wait_ge(wt_ps, m + 1)
                    if h >= 2:
                        act.wait_ge(wpv, h - 1)
                    b0 = 10 * (h % 2) + 4 * i
                    A(wa_pt[:, b0:b0 + nb, :], ps[:, m % 2, 0:nb * P].rearrange("p (b q) -> p b q", b=nb),
                      F.Copy).then_inc(wpt_done, 1)

            def wa_out(h):
                act.wait_ge(wpv, h + 1)
                r = slice(64 * (h % 2), 64 * (h % 2) + 64)
                A(o_wa[r, h // 2, :], ps[r, 2 + h % 2, :], F.Copy).then_inc(wO_ev, 1)

            act.wait_ge(in_small, 96)
            for u in range(WA_H + 2):
                if u < WA_H:
                    act.wait_ge(wnm_done, u + 1)
                    for qb in range(4):
                        c0, c1 = (P if qb == 0 else 0), (256 if qb == 3 else 384)
                        v = wa_p[:, u % 2, qb, c0:c1]
                        A(v, v, F.Exp, bias=nmx[:, u % 2, qb:qb + 1], accum_out=lsum[:, u % 2, qb:qb + 1])
                    A(esink[:, u % 2, :], nmx[:, u % 2, :], F.Exp, bias=sink[:, u:u + 1]).then_inc(we_done, 1)
                if 1 <= u <= WA_H:
                    wa_copy(u - 1)
                if u >= 2:
                    wa_out(u - 2)

            act.wait_ge(in_mem, 16)
            norm(3, memt, junk[:, :])
            norm_out(3, memT, MEMG, MEM)
            for n in range(PJ_XA + 12, PJ_XA + 20):
                act.wait_ge(pj_ps, n + 1)
                A(xa_q[:, n - PJ_XA - 12, :], ps[:, n % 4, :], F.Copy, scale=0.0625).then_inc(pjA, 1)
            for u in range(XA_H + 1):
                if u < XA_H:
                    if u >= 2:
                        act.wait_ge(xt_ps, 2 * (u - 1))
                    for qb in range(4):
                        act.wait_ge(xnm_done, 4 * u + qb + 1)
                        A(xa_p[:, u % 2, qb, :], ps[:, 4 + qb, 0:MEM], F.Exp, bias=nmx[:, u % 2, qb:qb + 1],
                          accum_out=lsum[:, u % 2, qb:qb + 1]).then_inc(xe1_done, 1)
                if u:
                    h = u - 1
                    for kb in range(2):
                        act.wait_ge(xt_ps, 2 * h + kb + 1)
                        if h >= 2:
                            act.wait_ge(xpv, 2 * (h - 1))
                        A(xa_pt[:, 2 * (h % 2) + kb, :], ps[:, kb, :], F.Copy).then_inc(xpt_done, 1)

            for n in range(NB * KT):
                act.wait_ge(g_ps, 2 * n + 1)
                if n >= 2:
                    act.wait_ge(m_done, n - 1)
                A(sg[:, n % 2, :], ps[:, 2 * (n % 4), :], F.Sigmoid).then_inc(gsig, 1)

            act.wait_ge(x3_done, 8)
            act.dma_start(h2g, I["ffn_norm_g_2"].partition_broadcast(P).rearrange("p a d -> p (a d)")).then_inc(in_moe, 16)
            act.dma_start(fing, I["final_norm_g_2"].partition_broadcast(P)).then_inc(in_moe, 16)
            norm(4, x, junk)
            norm_out(4, hT, FFN2G, S)
            act.wait_ge(lg_done, 1)
            A(lg, lg, F.Exp).then_inc(lexp, 1)
            with act.Fori(0, PAIRS) as q:
                for a in range(2):
                    act.wait_ge(e_chunks, q * ECH + (24 * a + 16))
                    for i in range(2):
                        act.wait_ge(ae_done, q * 4 + (2 * a + i + 1))
                        A(sg_e[64:128, i * 1024:i * 1024 + 1024],
                          ps[0:CAP, 2 * i:2 * i + 2, :].rearrange("p b n -> p (b n)"), F.Silu).then_inc(sg_done, 1)
            act.wait_ge(b67_free, PAIRS * SEQ + 2)
            for t in range(TT):
                if t:
                    act.wait_ge(f_sq, t)
                A(junk, x[:, t, :], F.Square, accum_out=ssq[:, t:t + 1]).then_inc(f_sq, 1)
            act.wait_ge(f_sq, TT)
            A(ssq[:], ssq[:], F.Sqrt, bias=epsb[:], scale=1.0 / D).then_inc(f_rt, 1)

        @block.vector
        def _(dve):
            V = nc.vector
            n_ = [0]

            def link(ins):
                n_[0] += 1
                ins.then_inc(dve_c, 1)
                dve.wait_ge(dve_c, n_[0])

            dve.wait_ge(m2i_ready, 1)
            link(V.tensor_scalar(m2i, m2i, 3, None, ALU.bitwise_and))
            V.tensor_scalar(mask[:, 3, :], m2i, 0.0, NEG, ALU.is_gt, ALU.mult).then_inc(m2_ready, 1)

            def norm(k, src, dst):
                nt = NORM_TILES[k]
                dve.wait_ge(n_rt, k + 1)
                link(V.reciprocal(rstd[:, 0:nt], ssq[:, 0:nt]))
                for t in range(nt):
                    V.tensor_scalar(dst[:, t, :], src[:, t, :], rstd[:, t:t + 1], None, ALU.mult).then_inc(n_xn, 1)

            def norm_out(k, dst, gain, ntok):
                for kb in range(1, KT, 2):
                    dve.wait_ge(n_tp, 8 * k + kb + 1)
                    V.tensor_scalar(dst[:, kb, :], ps[:, kb % 4, 0:ntok], vec[:, gain + kb:gain + kb + 1], None,
                                    ALU.mult).then_inc(n_evD, 1)

            dve.wait_ge(vec_ps, 1)
            link(V.tensor_copy(vec[:], ps[:, 7, 0:NVEC]))
            V.tensor_scalar(vec[:, QG:QG + 3], vec[:, QG:QG + 3], DH ** -0.5, None, ALU.mult)
            V.tensor_scalar(vec[:, SUBG:SUBG + 1], vec[:, SUBG:SUBG + 1], 0.8, None, ALU.mult).then_inc(vec_done, 1)
            norm(0, x, xn)
            dve.wait_ge(vec_done, 1)
            norm_out(0, hT, MIXG, S)

            dve.wait_ge(masks_done, 1)
            for g in range(GROUPS):
                for b in range(8):
                    n = 8 * g + b
                    gain = (QG if b < 4 else KG) + g
                    dve.wait_ge(rt_done, n + 1)
                    V.reciprocal(rr[:, n % 2, :], rt[:, n % 2, :]).then_inc(rr_done, 1)
                    dve.wait_ge(rr_done, n + 1)
                    o, a, r = qk[:, b, :], ps[:, n % 4, :], rr[:, n % 2, :]
                    if g:
                        o = o.rearrange("p (c j) -> p j c", c=4)
                        a, r = (v.rearrange("p (j c) -> p j c", c=4) for v in (a, r))
                    V.scalar_tensor_tensor(out=o, in0=a, scalar=vec[:, gain:gain + 1], in1=r,
                                           op0=ALU.mult, op1=ALU.mult).then_inc(qk_done, 1)
                for u in range(UB[g], UB[g + 1] + 1):
                    if u < UB[g + 1]:
                        _, h, tiles = units[u]
                        nt = len(tiles)
                        mrow = (0 if tiles[0] == 0 else 1) if g == 0 else g + 1
                        dve.wait_ge(s_ps, u + 1)
                        if u >= 3:
                            dve.wait_ge(t_ps, u - 2)
                        V.tensor_tensor(sm[:, u % 3, :], ps[:, 4 + u % 3, :], mask[:, mrow, :],
                                        ALU.add).then_inc(sm_done, 1)
                        dve.wait_ge(sm_done, u + 1)
                        V.tensor_reduce(nm1[:, g, tiles[0]:tiles[0] + nt, h],
                                        sm[:, u % 3, :].rearrange("p (t k) -> p t k", t=nt), AX.X, ALU.max,
                                        negate=True).then_inc(nm_done, 1)
                    m = u - 1
                    if m >= UB[g]:
                        dve.wait_ge(t_ps, m + 1)
                        if m >= 2:
                            dve.wait_ge(pv_done, m - 1)
                        V.tensor_copy(pt1[:, m % 2, :], ps[:, m % 2, :]).then_inc(pt_done, 1)
            for i in range(6):
                g = i % 3
                dve.wait_ge(r_ps, i + 1)
                o, a = rows[:, i, :], ps[0:HEADS1, i, :]
                if g:
                    o = o.rearrange("p (j c) -> p c j", c=4)
                    a = a.rearrange("p (c j) -> p c j", c=4)
                link(V.tensor_copy(o, a))
            dve.wait_ge(pv_done, UB[3])
            link(V.tensor_tensor(crow[:, 0, :], rows[:, 0, :], rows[:, 1, :], ALU.min))
            link(V.tensor_tensor(crow[:, 0, :], crow[:, 0, :], rows[:, 2, :], ALU.min))
            for g in range(GROUPS):
                last = V.tensor_tensor(coef[:, g, :], crow[:, 0, :], rows[:, g, :], ALU.subtract)
            last.then_inc(rowd, 1)
            dve.wait_ge(rowexp, 1)
            for g in range(GROUPS):
                last = V.tensor_tensor(rows[:, 3 + g, :], rows[:, 3 + g, :], coef[:, g, :], ALU.mult)
            link(last)
            link(V.tensor_tensor(crow[:, 0, :], rows[:, 3, :], rows[:, 4, :], ALU.add))
            link(V.tensor_tensor(crow[:, 0, :], crow[:, 0, :], rows[:, 5, :], ALU.add))
            link(V.reciprocal(crow[:, 1, :], crow[:, 0, :]))
            for g in range(GROUPS):
                last = V.tensor_tensor(coef[:, g, :], coef[:, g, :], crow[:, 1, :], ALU.mult)
            last.then_inc(coef_done, 1)
            dve.wait_ge(o_ev, 24)
            for n in range(12):
                b, g = n // 3, n % 3
                dve.wait_ge(bc_ps, n + 1)
                o = oT[:, b, :] if g == 0 else ctmp[:, n % 2, :]
                V.tensor_tensor(o, ps[:, 6 + n % 2, :], U[:, g, b, :], ALU.mult).then_inc(bc_done, 1)
                dve.wait_ge(bc_done, n + 1)
                if g:
                    link(V.tensor_tensor(oT[:, b, :], oT[:, b, :], ctmp[:, n % 2, :], ALU.add))
            dve.sem_inc(bc_done, 1)

            def residual(sem_ps, sem_done, banks):
                for n in range(8):
                    half, t = n // 4, n % 4
                    dve.wait_ge(sem_ps, n + 1)
                    xv = x[:, t, half * 512:half * 512 + 512]
                    V.tensor_tensor(xv, ps[:, banks(t, half), :], xv, ALU.add).then_inc(sem_done, 1)

            residual(wo_ps, x1_done, lambda t, half: t)

            norm(1, x, xn)
            norm_out(1, hT, FFNG, S)
            for j in range(FB + 1):
                if j < FB:
                    dve.wait_ge(f_id, 2 * j + 2)
                    cs = 4 * j
                    for k, sh in ((1, 1), (0, 2)):
                        for i, buf in enumerate((cg, cu)):
                            v = buf[:, j % 2, sh:]
                            if sh == 2:
                                dve.wait_ge(conv_done, cs + i + 1)
                            V.scalar_tensor_tensor(
                                out=v, in0=ps[:, 2 * (j % 2) + i, 0:S - sh],
                                scalar=vec[:, CW + 44 * k + 22 * i + j:CW + 44 * k + 22 * i + j + 1],
                                in1=v, op0=ALU.mult, op1=ALU.add).then_inc(conv_done, 1)
                if j:
                    m = j - 1
                    dve.wait_ge(silu_done, m + 1)
                    dve.wait_ge(conv_done, 4 * m + 4)
                    V.tensor_tensor(actT[:, m, :], cg[:, m % 2, :], cu[:, m % 2, :], ALU.mult).then_inc(act_done, 1)
            residual(dn_ps, x2_done, lambda t, half: 2 * t + half)

            norm(2, x, xn)
            norm_out(2, hT, ATTG, S)
            for n in range(8, 24):
                if PJ[n] == "D":
                    dve.wait_ge(pj_ps, n + 1)
                    if n < 16:
                        V.tensor_copy(da_k[:, n - 8, :], ps[:, n % 4, :]).then_inc(pjD, 1)
                    else:
                        t, half = (n - 16) % 4, (n - 16) // 4
                        V.tensor_copy(da_v[:, t, half * 512:half * 512 + 512], ps[:, n % 4, :]).then_inc(pjD, 1)
            dve.wait_ge(in_small, 96)
            for i in range(2):
                last = V.tensor_tensor_reduce(out=lamv[:, 2 * i, :], in0=lamv[:, 2 * i, :], in1=lamv[:, 2 * i + 1, :],
                                              scale=1.0, scalar=0.0, op0=ALU.mult, op1=ALU.add,
                                              accum_out=lamsc[:, i:i + 1])
            last.then_inc(lam_sum, 1)
            dve.wait_ge(lam_exp, 1)
            link(V.tensor_tensor(lamsc[:, 2:3], lamsc[:, 1:2], lamsc[:, 0:1], ALU.subtract))
            link(V.tensor_scalar(lamsc[:, 3:4], lamsc[:, 2:3], -0.2, None, ALU.add))

            def da_probs(u):
                dve.wait_ge(de_done, u + 1)
                link(V.reciprocal(rl[:, u % 2, :], lsum[:, u % 2, :]))
                c1 = rl[:, u % 2, :].rearrange("p (q m) -> p q m", m=2)[:, :, 1]
                link(V.tensor_scalar(c1, c1, lamsc[:, 3:4], None, ALU.mult))
                for i in range(2):
                    e0, e1 = da_e[:, u % 2, 2 * i, :], da_e[:, u % 2, 2 * i + 1, :]
                    link(V.tensor_scalar(e0, e0, rl[:, u % 2, 2 * i:2 * i + 1], None, ALU.mult))
                    last = V.scalar_tensor_tensor(out=e0, in0=e1, scalar=rl[:, u % 2, 2 * i + 1:2 * i + 2], in1=e0,
                                                  op0=ALU.mult, op1=ALU.add)
                last.then_inc(a_done, 1)

            for u in range(17):
                if u < 16:
                    h = u // 2
                    if u % 2 == 0:
                        dve.wait_ge(al_done, h + 1)
                    if u >= 2:
                        dve.wait_ge(dt_ps, 2 * (u - 1))
                    for i in range(4):
                        qb = 2 * (u % 2) + i // 2
                        dve.wait_ge(sd_ps, 4 * u + i + 1)
                        V.tensor_tensor_reduce(out=da_e[:, u % 2, i, :], in0=ps[:, 4 + i, :],
                                               in1=alibi[:, h % 2, 384 - P * qb:896 - P * qb], scale=1.0,
                                               scalar=-3e38, op0=ALU.add, op1=ALU.max,
                                               accum_out=mx[:, u % 2, i:i + 1]).then_inc(sd_done, 1)
                    dve.wait_ge(sd_done, 4 * u + 4)
                    V.tensor_scalar(nmx[:, u % 2, :], mx[:, u % 2, :], -1.0, None, ALU.mult).then_inc(dnm_done, 1)
                if u:
                    da_probs(u - 1)
            for h in range(8):
                dve.wait_ge(on_rt, h + 1)
                V.reciprocal(da_e[:, 1, h % 2, :], da_e[:, 0, 2 + h % 2, :]).then_inc(on_rr, 1)
                dve.wait_ge(on_rr, h + 1)
                V.scalar_tensor_tensor(out=o_da[:, h, :], in0=o_da[:, h, :], scalar=vec[:, SUBG:SUBG + 1],
                                       in1=da_e[:, 1, h % 2, :], op0=ALU.mult, op1=ALU.mult).then_inc(on_done, 1)

            for n in range(PJ_WA, PJ_XA):
                if PJ[n] == "D":
                    m = n - PJ_WA
                    dve.wait_ge(pj_ps, n + 1)
                    if m < 10:
                        for i in range(2):
                            for o in range(2):
                                last = V.tensor_copy(wa_k[64 * o:64 * o + 64, 2 * (m - 8) + i, :],
                                                     ps[64 * i:64 * i + 64, n % 4, :])
                        last.then_inc(pjD, 1)
                    else:
                        V.tensor_copy(wa_v[:, m - 10, :], ps[:, n % 4, 0:256]).then_inc(pjD, 1)

            def wa_probs(h):
                dve.wait_ge(we_done, h + 1)
                link(V.tensor_tensor(lsum[:, h % 2, :], lsum[:, h % 2, :], esink[:, h % 2, :], ALU.add))
                link(V.reciprocal(rl[:, h % 2, :], lsum[:, h % 2, :]))
                for qb in range(4):
                    c0, c1 = (P if qb == 0 else 0), (256 if qb == 3 else 384)
                    v = wa_p[:, h % 2, qb, c0:c1]
                    last = V.tensor_scalar(v, v, rl[:, h % 2, qb:qb + 1], None, ALU.mult)
                last.then_inc(aw_done, 1)

            for u in range(WA_H + 1):
                if u < WA_H:
                    dve.wait_ge(wal_done, u + 1)
                    if u >= 2:
                        dve.wait_ge(wt_ps, 3 * (u - 1))
                    for qb in range(4):
                        c0, c1 = (P if qb == 0 else 0), (256 if qb == 3 else 384)
                        dve.wait_ge(sw_ps, 4 * u + qb + 1)
                        V.tensor_tensor_reduce(out=wa_p[:, u % 2, qb, c0:c1], in0=ps[:, 4 + qb, c0:c1],
                                               in1=walibi[:, u % 2, c0:c1], scale=1.0, scalar=-3e38,
                                               op0=ALU.add, op1=ALU.max,
                                               accum_out=mx[:, u % 2, qb:qb + 1]).then_inc(sw_done, 1)
                    dve.wait_ge(sw_done, 4 * u + 4)
                    V.tensor_scalar(nmx[:, u % 2, :], mx[:, u % 2, :], sink[:, u:u + 1], -1.0, ALU.max,
                                    ALU.mult).then_inc(wnm_done, 1)
                if u:
                    wa_probs(u - 1)

            norm(3, memt, memn)
            norm_out(3, memT, MEMG, MEM)
            for n in range(PJ_XA, PJ_XA + 12):
                m = n - PJ_XA
                dve.wait_ge(pj_ps, n + 1)
                if m < 8:
                    V.tensor_copy(mkT[:, m, :], ps[:, n % 4, 0:MEM]).then_inc(pjD, 1)
                else:
                    t, half = (m - 8) % 2, (m - 8) // 2
                    V.tensor_copy(mv[:, t, half * 512:half * 512 + 512], ps[:, n % 4, :]).then_inc(pjD, 1)
            for u in range(XA_H + 2):
                if u < XA_H:
                    for qb in range(4):
                        dve.wait_ge(sx_ps, 4 * u + qb + 1)
                        V.tensor_reduce(nmx[:, u % 2, qb:qb + 1], ps[:, 4 + qb, 0:MEM], AX.X, ALU.max,
                                        negate=True).then_inc(xnm_done, 1)
                if 1 <= u <= XA_H:
                    h = u - 1
                    dve.wait_ge(xe1_done, 4 * h + 4)
                    link(V.reciprocal(rl[:, h % 2, :], lsum[:, h % 2, :]))
                    for qb in range(4):
                        v = xa_p[:, h % 2, qb, :]
                        last = V.tensor_scalar(v, v, rl[:, h % 2, qb:qb + 1], None, ALU.mult)
                    last.then_inc(ax_done, 1)
                if u >= 2:
                    h = u - 2
                    for i in range(2):
                        dve.wait_ge(xpv, 2 * h + i + 1)
                        V.tensor_copy(o_xa[:, 2 * h + i, :], ps[:, 2 + i, :]).then_inc(xO_ev, 1)

            for n in range(NB * KT):
                jj, b, sub = n // 6, n // 2 % 3, n % 2
                mv_ = merged[:, 2 * jj + sub, :]
                dve.wait_ge(gsig, n + 1)
                dve.wait_ge(g_ps, 2 * n + 2)
                if b == 0:
                    V.tensor_tensor(mv_, ps[:, 2 * (n % 4) + 1, :], sg[:, n % 2, :], ALU.mult).then_inc(m_done, 1)
                else:
                    link(V.tensor_tensor(gtmp[:, n % 2, :], ps[:, 2 * (n % 4) + 1, :], sg[:, n % 2, :], ALU.mult))
                    V.tensor_tensor(mv_, mv_, gtmp[:, n % 2, :], ALU.add).then_inc(m_done, 1)
            residual(wo2_ps, x3_done, lambda t, half: t)

            norm(4, x, xn)
            norm_out(4, hT, FFN2G, S)
            dve.wait_ge(in_moe, 32)
            for t in range(TT):
                V.tensor_tensor(h2[:, t, :], xn[:, t, :], h2g, ALU.mult).then_inc(h2_done, 1)
            dve.wait_ge(rt_ps, 1)
            lps = ps[:, 4, 0:TT * NE].rearrange("p (t e) -> p t e", t=TT)
            link(V.tensor_reduce(small[:, 0:4], lps, AX.X, ALU.max))
            V.tensor_tensor(lg, lps, small[:, 0:4].unsqueeze(2).to_broadcast([P, TT, NE]),
                            ALU.subtract).then_inc(lg_done, 1)
            dve.wait_ge(lexp, 1)
            link(V.reduce_sum(small[:, 4:8], lg, AX.X))
            link(V.reciprocal(small[:, 8:12], small[:, 4:8]))
            V.tensor_tensor(aff, lg, small[:, 8:12].unsqueeze(2).to_broadcast([P, TT, NE]),
                            ALU.mult).then_inc(affd, 1)
            dve.wait_ge(affT_ps, 1)
            V.tensor_copy(affT, ps[0:NE, 5, :])
            link(V.tensor_copy(wk, ps[0:NE, 5, :]))
            for r in range(8):
                link(V.max(out=top[:, 8 * r:8 * r + 8], in_=wk))
                if r < 7:
                    link(V.match_replace(out=wk, in_to_replace=top[:, 8 * r:8 * r + 8], in_values=wk, imm_value=-1.0))
            least, count = top[:, CAP - 1:CAP], small[0:NE, 12:13]
            dve.wait_ge(slots_ready, 1)
            V.tensor_scalar(gt, affT, least, 0.0, ALU.is_gt, ALU.add, accum_out=count)
            link(V.tensor_scalar(eq, affT, least, None, ALU.is_equal))
            link(V.tensor_tensor_scan(cum, ones, eq, 0.0, ALU.mult, ALU.add))
            link(V.tensor_scalar(small[0:NE, 13:14], count, -1.0, float(CAP), ALU.mult, ALU.add))
            link(V.scalar_tensor_tensor(out=eq, in0=cum, scalar=small[0:NE, 13:14], in1=eq, op0=ALU.is_le, op1=ALU.mult))
            link(V.tensor_tensor(gt, gt, eq, ALU.add))
            link(V.tensor_tensor_scan(cum, ones, gt, 0.0, ALU.mult, ALU.add))
            V.tensor_tensor(wk, gt, cum, ALU.mult).then_inc(slot_d, 1)
            dve.wait_ge(slot_ps, 1)
            link(V.tensor_copy(slotT, ps[:, 6, 0:TT * NE].rearrange("p (t e) -> p t e", t=TT)))
            for t in range(TT):
                V.tensor_tensor(OH[:, t, :].rearrange("p (e c) -> p e c", e=NE),
                                iota1.unsqueeze(1).to_broadcast([P, NE, CAP]),
                                slotT[:, t, :].unsqueeze(2).to_broadcast([P, NE, CAP]),
                                ALU.is_equal).then_inc(oh_done, 1)
            for q in range(PAIRS):
                dve.wait_ge(og_ps, q + 1)
                V.tensor_copy(ohgT[:, q, :], ps[:, q % 4, :]).then_inc(og_ev, 1)

            dve.wait_ge(og_ev, PAIRS)
            dve.sem_inc(b67_free, 2)
            dve.sem_inc(ae_done, 2)
            dve.sem_inc(ye_done, 1)
            with dve.Fori(0, PAIRS) as q:
                V.tensor_copy(ohst, ohgT[:, q, :]).then_inc(st_done, 1)
                for i in range(2):
                    dve.wait_ge(ga_ps, q * 2 + (i + 1))
                    V.tensor_copy(xeT[:, 4 * i:4 * i + 4, :].rearrange("p k c -> p (k c)"),
                                  ps[:, 6 + i, :]).then_inc(b67_free, 1)
                for a in range(2):
                    for i in range(2):
                        dve.wait_ge(sg_done, q * 4 + (2 * a + i + 1))
                        V.tensor_tensor(act_tok[64 * i:64 * i + 64, :],
                                        ps[64:128, 2 * i:2 * i + 2, :].rearrange("p b n -> p (b n)"),
                                        sg_e[64:128, i * 1024:i * 1024 + 1024], ALU.mult).then_inc(ae_done, 1)
                    for i in range(2):
                        dve.wait_ge(tr_ps, q * 4 + (2 * a + i + 1))
                        V.tensor_copy(act_e.rearrange("p (h j) c -> p j h c", h=2)[:, 4 * i:4 * i + 4, :, :],
                                      ps[:, 6 + i, :].rearrange("p (j h c) -> p j h c", j=4, h=2)).then_inc(b67_free, 1)
                    dve.wait_ge(e_chunks, q * ECH + (24 * a + 24))
                    V.tensor_copy(Y[64 * a:64 * a + 64, 0:512], ps[0:64, 4, :])
                    V.tensor_copy(Y[64 * a:64 * a + 64, 512:1024], ps[64:128, 4, :]).then_inc(ye_done, 1)
                for i in range(8):
                    t, half = i // 2, i % 2
                    xv = x[:, t, half * 512:half * 512 + 512]
                    dve.wait_ge(c_ps, q * 8 + (i + 1))
                    V.tensor_tensor(xv, ps[:, 6 + half, :], xv, ALU.add).then_inc(b67_free, 1)
            dve.wait_ge(f_rt, 1)
            link(V.reciprocal(rstd[:], ssq[:]))
            for t in range(TT):
                V.scalar_tensor_tensor(out=xn2[:, t, :], in0=x[:, t, :], scalar=rstd[:, t:t + 1], in1=fing,
                                       op0=ALU.mult, op1=ALU.mult).then_inc(o_done, 1)

        @block.tensor
        def _(pe):
            mm = nc.tensor.matmul
            at = [0]

            def take(k):
                c = at[0]
                at[0] += 1
                pe.wait_ge(landed[c % NS], 16 * (c // NS + 1))
                return ring[:, c % NS, :].rearrange("p (k n) -> p k n", k=k)

            def norm_T(k, src, ntile):
                pe.wait_ge(n_xn, nbase[k + 1])
                for kb in range(KT):
                    if kb >= 4:
                        pe.wait_ge(n_evD if kb % 2 else n_evA, 4 * k + (kb - 4) // 2 + 1)
                    for t in range(ntile):
                        last = nc.tensor.transpose(ps[:, kb % 4, t * P:(t + 1) * P], src[:, t, kb * P:(kb + 1) * P], ident[:])
                    last.then_inc(n_tp, 1)

            def norm_ready(k):
                pe.wait_ge(n_evA, 4 * (k + 1))
                pe.wait_ge(n_evD, 4 * (k + 1))

            pe.wait_ge(consts, 1)
            pe.wait_ge(in_vec, 16 * 13)
            for i, (c0, n) in enumerate(((0, 84), (84, 88), (172, 44), (216, 7))):
                last = nc.tensor.transpose(ps[:, 7, c0:c0 + n], vrow[0:n, i, :], ident[0:n, 0:n])
            last.then_inc(vec_ps, 1)
            norm_T(0, xn, TT)
            norm_ready(0)

            for g in range(GROUPS):
                if g:
                    pe.wait_ge(o_ev, 8 * g)
                for b in range(9):
                    n = 8 * g + b
                    if b < 8:
                        if b % 2 == 0:
                            w = take(KT)
                        if n >= 4:
                            pe.wait_ge(qk_done, n - 3)
                        for k in range(KT):
                            last = mm(ps[:, n % 4, :], w[:, k, (b % 2) * P:(b % 2) * P + P], hT[:, k, :],
                                      start=(k == 0), stop=(k == KT - 1))
                        last.then_inc(qk_ps, 1)
                    if b:
                        m = n - 1
                        pe.wait_ge(sq_done, m + 1)
                        if m >= 2:
                            pe.wait_ge(rt_done, m - 1)
                        mm(ps[:, 6 + m % 2, :], mean64[:], sq[:, m % 2, :], start=True, stop=True).then_inc(ssq_ps, 1)
                wv = [take(4), take(4)]
                for t in range(TT):
                    if t == 2:
                        pe.wait_ge(rt_done, 8 * (g + 1))
                    for k in range(KT):
                        lhsT = hT[:, k, t * P:(t + 1) * P] if g == 0 else hT[:, k, t::4]
                        last = mm(ps[:, 4 + t, :], lhsT, wv[k // 4][:, k % 4, :], start=(k == 0), stop=(k == KT - 1))
                    last.then_inc(v_ps, 1)
                pe.wait_ge(qk_done, 8 * (g + 1))
                pe.wait_ge(v_ev, TT * (g + 1))
                for u in range(UB[g], UB[g + 1] + 2):
                    if u < UB[g + 1]:
                        _, h, tiles = units[u]
                        r = slice(64 * (h % 2), 64 * (h % 2) + 64)
                        if u - 3 >= UB[g]:
                            pe.wait_ge(sm_done, u - 2)
                        for i, t in enumerate(tiles):
                            q = qk[r, h // 2, t * P:(t + 1) * P]
                            if g == 0:
                                for s in range(2):
                                    kb = max(t - 1 + s, 0)
                                    last = mm(ps[:, 4 + u % 3, (2 * i + s) * P:(2 * i + s + 1) * P], q,
                                              qk[r, 4 + h // 2, kb * P:(kb + 1) * P], start=True, stop=True)
                            else:
                                last = mm(ps[:, 4 + u % 3, i * P:(i + 1) * P], q,
                                          qk[r, 4 + h // 2, t * P:(t + 1) * P], start=True, stop=True)
                        last.then_inc(s_ps, 1)
                    m = u - 1
                    if UB[g] <= m < UB[g + 1]:
                        pe.wait_ge(p_done, m + 1)
                        if m - 2 >= 0:
                            pe.wait_ge(pt_done, m - 1)
                        for i in range(4):
                            last = nc.tensor.transpose(ps[:, m % 2, i * P:(i + 1) * P], sm[:, m % 3, i * P:(i + 1) * P], ident[:])
                        last.then_inc(t_ps, 1)
                    m = u - 2
                    if m >= UB[g]:
                        _, h, tiles = units[m]
                        r = slice(64 * (h % 2), 64 * (h % 2) + 64)
                        pe.wait_ge(pt_done, m + 1)
                        if 8 * g + h >= 2:
                            pe.wait_ge(o_ev, 8 * g + h - 1)
                        for i, t in enumerate(tiles):
                            o = ps[r, 2 + h % 2, t * P:(t + 1) * P]
                            if g == 0:
                                for s in range(2):
                                    kb = max(t - 1 + s, 0)
                                    last = mm(o, v1[:, kb, h * DH:(h + 1) * DH], pt1[:, m % 2, (2 * i + s) * P:(2 * i + s + 1) * P],
                                              start=(s == 0), stop=(s == 1))
                            else:
                                last = mm(o, v1[:, t, h * DH:(h + 1) * DH], pt1[:, m % 2, i * P:(i + 1) * P], start=True, stop=True)
                        last.then_inc(pv_done, 1)
            pe.wait_ge(o_ev, 24)
            for i in range(6):
                stat, g = (nm1, l1)[i // 3], i % 3
                for t in range(TT):
                    last = nc.tensor.transpose(ps[0:HEADS1, i, t * P:(t + 1) * P], stat[:, g, t, :], ident[:])
                last.then_inc(r_ps, 1)
            pe.wait_ge(coef_done, 1)
            for n in range(12):
                b, g = n // 3, n % 3
                if n >= 2:
                    pe.wait_ge(bc_done, n - 1)
                mm(ps[:, 6 + n % 2, :], selB[:, b, :], coef[:, g, :], start=True, stop=True).then_inc(bc_ps, 1)

            def out_proj(oT_, nk, sem_ps, done):
                for half in range(2):
                    w = [take(4) for _ in range(nk // 4)]
                    for t in range(TT):
                        if half:
                            pe.wait_ge(done, t + 1)
                        for k in range(nk):
                            last = mm(ps[:, t, :], oT_[:, k, t * P:(t + 1) * P], w[k // 4][:, k % 4, :],
                                      start=(k == 0), stop=(k == nk - 1))
                        last.then_inc(sem_ps, 1)

            pe.wait_ge(bc_done, 13)
            out_proj(oT, 4, wo_ps, x1_done)

            norm_T(1, xn, TT)
            norm_ready(1)
            for j in range(FB):
                if j % 2 == 0:
                    w = [take(KT), take(KT)]
                if j >= 2:
                    pe.wait_ge(conv_done, 4 * (j - 1))
                for i in range(2):
                    for k in range(KT):
                        last = mm(ps[:, 2 * (j % 2) + i, :], w[i][:, k, (j % 2) * P:(j % 2) * P + P], hT[:, k, :],
                                  start=(k == 0), stop=(k == KT - 1))
                    last.then_inc(f_ps, 1)
            pe.wait_ge(conv_done, 4 * FB)
            for f in range(FB):
                if f % 2 == 0:
                    w = take(2)
                pe.wait_ge(act_done, f + 1)
                for half in range(2):
                    for t in range(TT):
                        last = mm(ps[:, 2 * t + half, :], actT[:, f, t * P:(t + 1) * P], w[:, f % 2, half * 512:half * 512 + 512],
                                  start=(f == 0), stop=(f == FB - 1))
                        if f == FB - 1:
                            last.then_inc(dn_ps, 1)
                if f % 2 and f < FB - 1:
                    last.then_inc(dn_w, 1)

            jobs = [0]

            def proj_T(nblk, rhs, ntok):
                for b in range(nblk):
                    if b % 2 == 0:
                        w = take(KT)
                    n = jobs[0]
                    jobs[0] += 1
                    pj_bank_free(pe, n)
                    for k in range(KT):
                        last = mm(ps[:, n % 4, 0:ntok], w[:, k, (b % 2) * P:(b % 2) * P + P], rhs[:, k, :],
                                  start=(k == 0), stop=(k == KT - 1))
                    last.then_inc(pj_ps, 1)

            def proj_tok(src, ntile, ncol):
                for half in range(max(ncol // 512, 1)):
                    w = [take(4), take(4)] if ncol >= 512 else [take(KT)]
                    nk = KT // len(w)
                    for t in range(ntile):
                        n = jobs[0]
                        jobs[0] += 1
                        pj_bank_free(pe, n)
                        for k in range(KT):
                            last = mm(ps[:, n % 4, 0:min(ncol, 512)], src[:, k, t * P:(t + 1) * P], w[k // nk][:, k % nk, :],
                                      start=(k == 0), stop=(k == KT - 1))
                        last.then_inc(pj_ps, 1)

            pe.wait_ge(x2_done, 8)
            norm_T(2, xn, TT)
            norm_ready(2)
            proj_T(16, hT, S)
            proj_tok(hT, TT, D)
            pj_all_done(pe, PJ_WA)

            def da_T(u):
                pe.wait_ge(a_done, u + 1)
                for i in range(2):
                    if u:
                        pe.wait_ge(dpt_done, 2 * (u - 1) + i + 1)
                    for kb in range(4):
                        last = nc.tensor.transpose(ps[:, i, kb * P:(kb + 1) * P], da_e[:, u % 2, 2 * i, kb * P:(kb + 1) * P], ident[:])
                    last.then_inc(dt_ps, 1)

            def da_pv(h):
                pe.wait_ge(dpt_done, 4 * h + 4)
                if h >= 2:
                    pe.wait_ge(dO_ev, h - 1)
                for kb in range(4):
                    last = mm(ps[:, 2 + h % 2, :], da_v[:, kb, h * P:(h + 1) * P], da_pt[:, 4 * (h % 2) + kb, :],
                              start=(kb == 0), stop=(kb == 3))
                last.then_inc(dpv, 1)

            for u in range(16 + 3):
                if u < 16:
                    for i in range(4):
                        h, qb, m = u // 2, 2 * (u % 2) + i // 2, i % 2
                        if u:
                            pe.wait_ge(sd_done, 4 * (u - 1) + i + 1)
                        mm(ps[:, 4 + i, :], da_q[64 * m:64 * m + 64, h, qb * P:(qb + 1) * P], da_k[64 * m:64 * m + 64, h, :],
                           start=True, stop=True).then_inc(sd_ps, 1)
                if 1 <= u <= 16:
                    da_T(u - 1)
                if u >= 3 and u % 2:
                    da_pv((u - 3) // 2)
            for h in range(8):
                pe.wait_ge(on_sq, h + 1)
                if h >= 2:
                    pe.wait_ge(on_rt, h - 1)
                mm(ps[:, 4 + h % 2, :], mean128[:], da_e[:, 0, h % 2, :], start=True, stop=True).then_inc(on_ps, 1)

            proj_T(10, hT, S)
            proj_tok(hT, TT, 256)
            pj_all_done(pe, PJ_XA)

            def wa_T(h):
                pe.wait_ge(aw_done, h + 1)
                for i in range(3):
                    m = 3 * h + i
                    if m >= 2:
                        pe.wait_ge(wpt_done, m - 1)
                    for j, (qb, kb) in enumerate(WA_BLOCKS[4 * i:4 * i + 4]):
                        c = (kb - qb + 1) * P
                        last = nc.tensor.transpose(ps[:, m % 2, j * P:(j + 1) * P], wa_p[:, h % 2, qb, c:c + P], ident[:])
                    last.then_inc(wt_ps, 1)

            def wa_pv(h):
                r = slice(64 * (h % 2), 64 * (h % 2) + 64)
                kv = h // 4
                pe.wait_ge(wpt_done, 3 * h + 3)
                if h >= 2:
                    pe.wait_ge(wO_ev, h - 1)
                for n, (qb, kb) in enumerate(WA_BLOCKS):
                    last = mm(ps[r, 2 + h % 2, qb * P:(qb + 1) * P], wa_v[:, kb, kv * 64:kv * 64 + 64],
                              wa_pt[:, 10 * (h % 2) + n, :], start=(kb == WA_KB[qb][0]), stop=(kb == WA_KB[qb][-1]))
                last.then_inc(wpv, 1)

            for u in range(WA_H + 2):
                if u < WA_H:
                    r = slice(64 * (u % 2), 64 * (u % 2) + 64)
                    for qb in range(4):
                        c0, c1 = (P if qb == 0 else 0), (256 if qb == 3 else 384)
                        k0 = (qb - 1) * P + c0
                        if u:
                            pe.wait_ge(sw_done, 4 * (u - 1) + qb + 1)
                        mm(ps[:, 4 + qb, c0:c1], wa_q[r, u // 2, qb * P:(qb + 1) * P], wa_k[r, u // 4, k0:k0 + c1 - c0],
                           start=True, stop=True).then_inc(sw_ps, 1)
                if 1 <= u <= WA_H:
                    wa_T(u - 1)
                if u >= 2:
                    wa_pv(u - 2)

            pe.wait_ge(wO_ev, WA_H)
            norm_T(3, memn, MEM // P)
            norm_ready(3)
            proj_T(8, memT, MEM)
            proj_tok(memT, MEM // P, D)
            proj_T(8, hT, S)
            pj_all_done(pe, PJ_XA + 20)
            for u in range(XA_H + 2):
                if u < XA_H:
                    for qb in range(4):
                        if u:
                            pe.wait_ge(xe1_done, 4 * (u - 1) + qb + 1)
                        for db in range(2):
                            last = mm(ps[:, 4 + qb, 0:MEM], xa_q[:, 2 * u + db, qb * P:(qb + 1) * P], mkT[:, 2 * u + db, :],
                                      start=(db == 0), stop=(db == 1))
                        last.then_inc(sx_ps, 1)
                if 1 <= u <= XA_H:
                    h = u - 1
                    pe.wait_ge(ax_done, h + 1)
                    for kb in range(2):
                        if h:
                            pe.wait_ge(xpt_done, 2 * (h - 1) + kb + 1)
                        for qb in range(4):
                            last = nc.tensor.transpose(ps[:, kb, qb * P:(qb + 1) * P], xa_p[:, h % 2, qb, kb * P:(kb + 1) * P], ident[:])
                        last.then_inc(xt_ps, 1)
                if u >= 2:
                    h = u - 2
                    pe.wait_ge(xpt_done, 2 * h + 2)
                    for i in range(2):
                        if h:
                            pe.wait_ge(xO_ev, 2 * (h - 1) + i + 1)
                        for kb in range(2):
                            last = mm(ps[:, 2 + i, :], mv[:, kb, h * 256 + i * P:h * 256 + (i + 1) * P],
                                      xa_pt[:, 2 * (h % 2) + kb, :], start=(kb == 0), stop=(kb == 1))
                        last.then_inc(xpv, 1)

            pe.wait_ge(on_done, 8)
            pe.wait_ge(xO_ev, 8)
            for n in range(NB * KT):
                b, sub = n // 2 % 3, n % 2
                o_b = (o_da, o_wa, o_xa)[b]
                if sub == 0:
                    w = [take(KT), take(KT)]
                if n >= 4:
                    pe.wait_ge(m_done, n - 3)
                for i, rhs in enumerate((hT, o_b)):
                    for k in range(KT):
                        last = mm(ps[:, 2 * (n % 4) + i, :], w[i][:, k, sub * P:sub * P + P], rhs[:, k, :],
                                  start=(k == 0), stop=(k == KT - 1))
                    last.then_inc(g_ps, 1)
            pe.wait_ge(m_done, NB * KT)
            out_proj(merged, KT, wo2_ps, x3_done)

            norm_T(4, xn, TT)
            norm_ready(4)
            pe.wait_ge(in_small, 96)
            for t in range(TT):
                for k in range(KT):
                    last = mm(ps[:, 4, t * NE:(t + 1) * NE], hT[:, k, t * P:(t + 1) * P], wr[:, k, :],
                              start=(k == 0), stop=(k == KT - 1))
            last.then_inc(rt_ps, 1)
            pe.wait_ge(affd, 1)
            for t in range(TT):
                last = nc.tensor.transpose(ps[0:NE, 5, t * P:(t + 1) * P], aff[:, t, :], ident[:])
            last.then_inc(affT_ps, 1)
            pe.wait_ge(slot_d, 1)
            for t in range(TT):
                last = nc.tensor.transpose(ps[:, 6, t * NE:(t + 1) * NE], wk[:, t * P:(t + 1) * P], ident[0:NE, 0:NE])
            last.then_inc(slot_ps, 1)
            pe.wait_ge(ohg_done, TT)
            for q in range(PAIRS):
                if q >= 4:
                    pe.wait_ge(og_ev, q - 3)
                for t in range(TT):
                    last = nc.tensor.transpose(ps[:, q % 4, t * P:(t + 1) * P], OHg[:, t, q * P:(q + 1) * P], ident[:])
                last.then_inc(og_ps, 1)
            pe.wait_ge(og_ev, PAIRS)
            pe.wait_ge(h2_done, TT)

            c0_ = at[0]
            assert c0_ == NCH

            def take_e(q, c):
                n = NCH + c
                pe.wait_ge(landed[n % NS], q * (16 * ECH // NS) + 16 * (n // NS + 1))
                return ring[:, n % NS, :]

            with pe.Fori(0, PAIRS) as q:
                for i in range(2):
                    pe.wait_ge(b67_free, q * SEQ + (i + 1))
                    for db in range(4):
                        for t in range(TT):
                            kb = 4 * i + db
                            last = mm(ps[:, 6 + i, db * P:(db + 1) * P], h2[:, t, kb * P:(kb + 1) * P],
                                      OH[:, t, bass.ds(q * P, P)], start=(t == 0), stop=(t == TT - 1))
                    last.then_inc(ga_ps, 1)
                pe.wait_ge(b67_free, q * SEQ + 4)
                for a in range(2):
                    pe.wait_ge(ae_done, q * 4 + (2 * a + 2))
                    for k in range(KT):
                        ws = [take_e(q, 24 * a + 2 * k), take_e(q, 24 * a + 2 * k + 1)]
                        for c in range(4):
                            for i, w in enumerate(ws):
                                last = mm(ps[64 * i:64 * i + 64, c, :], xeT[:, k, a * CAP:(a + 1) * CAP],
                                          w[:, c * 512:c * 512 + 512], start=(k == 0), stop=(k == KT - 1))
                                if c == 3:
                                    last.then_inc(e_chunks, 1)
                    for i in range(2):
                        pe.wait_ge(b67_free, q * SEQ + (2 * a + i + 3))
                        if i == 0:
                            pe.wait_ge(ae_done, q * 4 + (2 * a + 4))
                        for j in range(4):
                            f = 4 * i + j
                            last = nc.tensor.transpose(ps[:, 6 + i, j * P:(j + 1) * P], act_tok[:, f * P:(f + 1) * P], ident[:])
                        last.then_inc(tr_ps, 1)
                    pe.wait_ge(b67_free, q * SEQ + (2 * a + 6))
                    pe.wait_ge(ye_done, q * 2 + (a + 1))
                    for k in range(8):
                        w = take_e(q, 24 * a + 16 + k)
                        for j in range(2):
                            f = 2 * k + j
                            for half in range(2):
                                last = mm(ps[64 * half:64 * half + 64, 4, :], act_e[:, f, :],
                                          w[:, j * D + half * 512:j * D + half * 512 + 512],
                                          start=(f == 0), stop=(f == FT - 1))
                        last.then_inc(e_chunks, 1)
                pe.wait_ge(st_done, q + 1)
                pe.wait_ge(ye_done, q * 2 + 3)
                for i in range(8):
                    t, half = i // 2, i % 2
                    pe.wait_ge(b67_free, q * SEQ + (i + 7))
                    mm(ps[:, 6 + half, :], ohst[:, t * P:(t + 1) * P], Y[:, half * 512:half * 512 + 512],
                       start=True, stop=True).then_inc(c_ps, 1)


_INS = ["x", "mixer_norm", "ffn_norm", "attn_w_in", "attn_q_gain", "attn_k_gain", "attn_w_out",
        "ffn_w_up", "ffn_conv_w", "ffn_conv_b", "ffn_w_down", "mem_2", "attn_norm_g_2", "mem_norm_g_2",
        "w_in_2", "w_mem_kv_2", "da_lambda_q1_2", "da_lambda_k1_2", "da_lambda_q2_2", "da_lambda_k2_2",
        "da_subln_g_2", "wa_sink_2", "w_da_o_2", "w_wa_o_2", "w_xa_o_2", "w_out_2", "ffn_norm_g_2",
        "w_router_2", "w_exp_gate_2", "w_exp_up_2", "w_exp_down_2", "final_norm_g_2"]


def kernel(**inputs):
    import numpy as np
    import concourse.bacc as bacc
    from concourse import mybir
    from concourse.bass_utils import run_bass_kernel_spmd

    nc = bacc.Bacc("TRN2", target_bir_lowering=False, num_devices=1)
    arrays, aps = {}, {}
    for name in _INS:
        a = np.ascontiguousarray(inputs[name])
        arrays["in_" + name] = a
        aps[name] = nc.dram_tensor("in_" + name, a.shape, mybir.dt.from_np(a.dtype), kind="ExternalInput").ap()
    out = nc.dram_tensor("out_0", (1, S, D), mybir.dt.float32, kind="ExternalOutput").ap()
    build(nc, aps, out)
    r = run_bass_kernel_spmd(nc, [arrays], core_ids=[0])
    return r.results[0]["out_0"]
```

```python
import concourse.bass as bass
from concourse import mybir
from contextlib import ExitStack

S, D, P = 512, 1024, 128
TT, KT = S // P, D // P
EPS = 1e-6
NEG = -1e30
GROUPS, HEADS1, DH = 3, 8, 64
GW = HEADS1 * DH
FH, FB = 2816, 2816 // P
MEM = 256
DA_H, WA_H, WA_KV, XA_H, NB = 8, 16, 4, 4, 3
NE, CAP, FE = 16, 64, 2048
PAIRS, FT = NE // 2, FE // P
NS, SLOT = 8, 2048
RS = 4
HALF = SLOT // 2
COL = {}
_at = 0
for _n, _w in (("daq", 1024), ("dak", 1024), ("dav", 1024), ("waq", 1024), ("wak", 256),
               ("wav", 256), ("xaq", 1024), ("gate", 3072)):
    COL[_n] = _at
    _at += _w
MIXG, FFNG, ATTG, MEMG, FFN2G, CB, CW = 0, 8, 16, 24, 32, 40, 84
QG, KG, SUBG, NVEC = 216, 219, 222, 223
NORM_TILES = [TT, TT, TT, MEM // P, TT]
WA_KB = [[0, 1], [0, 1, 2], [1, 2, 3], [2, 3]]
WA_BLOCKS = [(qb, kb) for qb in range(4) for kb in WA_KB[qb]]


def build(nc, I, out):
    f32, f32r, i32 = mybir.dt.float32, mybir.dt.float32r, mybir.dt.int32
    ALU, ACT, AX = mybir.AluOpType, mybir.ActivationFunctionType, mybir.AxisListType
    ctx = ExitStack()
    with ctx:
        def sb(name, shape, dt=f32):
            return ctx.enter_context(nc.sbuf_tensor(name, shape, dt))

        def sem(name):
            return ctx.enter_context(nc.semaphore(name))

        def place(t, words):
            return t, nc.sbuf_base - 4 * words

        ring, ring_at = place(sb("ring", [P, NS, SLOT]), NS * SLOT)
        x = sb("x", [P, TT, D])
        hT, hT_at = place(sb("hT", [P, KT, S]), KT * S)
        arena, arena_at = place(sb("arena", [P, 27264]), 27264)
        one = sb("one", [P, 1])
        ident = sb("ident", [P, P])
        mean64 = sb("mean64", [P, P])
        mean128 = sb("mean128", [P, P])
        vec = sb("vec", [P, NVEC])
        wr = sb("wr", [P, KT, NE])
        epsb = sb("epsb", [P, 1])
        ssq = sb("ssq", [P, TT])
        rstd = sb("rstd", [P, TT])
        nm1 = sb("nm1", [P, GROUPS, TT, HEADS1])
        l1 = sb("l1", [P, GROUPS, TT, HEADS1])
        sink = sb("sink", [P, WA_H])
        lamsc = sb("lamsc", [P, 4])
        mx = sb("mx", [P, 2, 4])
        nmx = sb("nmx", [P, 2, 4])
        lsum = sb("lsum", [P, 2, 4])
        esink = sb("esink", [P, 2, 4])
        rl = sb("rl", [P, 2, 4])
        ps = ctx.enter_context(nc.psum_tensor("ps", [P, 8, 512], f32))

        def ar(off, *shape):
            n = 1
            for s in shape:
                n *= s
            v = arena[:, off:off + n]
            if len(shape) == 2:
                v = v.rearrange("p (a b) -> p a b", a=shape[0])
            elif len(shape) == 3:
                v = v.rearrange("p (a b c) -> p a b c", a=shape[0], b=shape[1])
            return v

        def part(name, base, off, *shape):
            return nc.alloc_sbuf_tensor_at(name, [P, *shape], f32r, offset=base + 4 * off)[:]

        w_hi = part("w_hi", ring_at, RS * SLOT, 2, HALF)
        w_lo = part("w_lo", ring_at, RS * SLOT + 2 * HALF, 2, HALF)
        h_hi = part("h_hi", hT_at, 0, KT, S)
        h_lo = part("h_lo", ring_at, RS * SLOT + 4 * HALF, KT, S)
        oT_hi = part("oT_hi", arena_at, 0, 4, S)
        oT_lo = part("oT_lo", arena_at, 2048, 4, S)
        act_hi = part("act_hi", arena_at, 0, FB, S)
        act_lo = part("act_lo", arena_at, 13312, FB, S)
        mem_hi = part("mem_hi", arena_at, 16384, KT, MEM)
        mem_lo = part("mem_lo", arena_at, 24576, KT, MEM)
        br_hi = part("br_hi", arena_at, 18432, KT, S)
        br_lo = part("br_lo", arena_at, 22528, KT, S)
        mg_hi = part("mg_hi", arena_at, 0, KT, S)
        mg_lo = part("mg_lo", arena_at, 4096, KT, S)

        qk = ar(0, 8, S)
        k1_odd = ar(23040, 4, S)
        v1 = ar(4096, TT, GW)
        U = ar(6144, GROUPS, 4, S)
        mask = ar(12288, 4, 512)
        sm = ar(14336, 3, 512)
        pt1 = ar(15872, 2, 512)
        sq = ar(16896, 2, 512)
        rt = ar(17920, 2, 512)
        rr = ar(18944, 2, 512)
        rows = ar(19968, 6, 512)[0:HEADS1]
        oT = ar(23040, 4, S)
        selB = ar(25088, 4, P)
        m2i = arena[:, 25600:26112].bitcast(i32)
        coef_all = ar(14336, 3, 512)
        coef = coef_all[0:HEADS1]
        crow = ar(15872, 2, 512)[0:HEADS1]
        ctmp = ar(16896, 2, 512)
        vrow = ar(0, 4, P)
        xn = ar(19968, TT, D)
        junk = ar(24064, D)
        junk2 = ar(24576, D)
        cg = ar(11264, 2, S)
        cu = ar(12288, 2, S)
        o_da, o_wa, o_xa = ar(0, KT, S), ar(4096, KT, S), ar(8192, KT, S)
        da_q, da_k, da_v = ar(12288, KT, S), ar(16384, KT, S), ar(20480, TT, D)
        da_k1 = ar(0, KT, S)
        o_raw = ar(16384, KT, S)
        da_e = ar(4096, 2, 4, S)
        da_pt = ar(8192, 8, S)
        dist = ar(24576, 896)
        alibi = ar(25472, 2, 896)
        lamv = ar(8192, 4, 64)
        wa_q, wa_k, wa_v = ar(12288, KT, S), ar(16384, WA_KV, S), ar(18432, TT, 256)
        wa_k1 = ar(10240, WA_KV, S)
        wa_p = ar(19456, 2, 4, 384)
        wa_pt = ar(22528, 20, P)
        wdist = ar(25600, 384)
        walibi = ar(25984, 2, 384)
        memt = ar(8192, 2, D)
        memn = ar(10240, 2, D)
        xa_q, mkT, mv = ar(12288, KT, S), ar(18432, KT, MEM), ar(20480, 2, D)
        xa_p = ar(22528, 2, 4, MEM)
        xa_pt = ar(24576, 4, S)
        merged = ar(12288, KT, S)
        sg = ar(16384, 2, S)
        gtmp = ar(17408, 2, S)
        h2 = ar(0, TT, D)
        OH = ar(4096, TT, NE * CAP)
        ohgT = ar(8192, PAIRS, S)
        xeT = ar(12288, KT, P)
        act_e = ar(13312, FT, CAP)
        Y = ar(14336, D)
        ohst = ar(15360, S)
        act_tok = ar(24064, FE // 2)
        sg_e = ar(25088, FE)
        h2g = ar(16896, D)
        fing = ar(17920, D)
        iota1 = ar(18944, CAP)
        aff = ar(19008, TT, NE)
        lg = ar(19072, TT, NE)
        slotT = ar(19136, TT, NE)
        small = ar(19200, 16)
        top = ar(19216, CAP)[0:NE]
        xn2 = ar(19968, TT, D)
        OHg = ar(19968, TT, NE * CAP)
        affT = ar(24096, S)[0:NE]
        wk = ar(24608, S)[0:NE]
        gt = ar(25120, S)[0:NE]
        eq = ar(25632, S)[0:NE]
        cum = ar(26144, S)[0:NE]
        ones = ar(26656, S)[0:NE]

        landed = [sem(f"landed{i}") for i in range(NS)]
        w_high, w_highA, w_split, w_used = (sem(n) for n in ("w_high", "w_highA", "w_split", "w_used"))
        e_chunks, slots_ready, tr_ps = sem("e_chunks"), sem("slots_ready"), sem("tr_ps")
        in_x = [sem(f"in_x{t}") for t in range(TT)]
        in_vec, in_small, in_moe, in_mem = sem("in_vec"), sem("in_small"), sem("in_moe"), sem("in_mem")
        pool_c, act_c, dve_c = sem("pool_chain"), sem("act_chain"), sem("dve_chain")
        consts, masks_done, m2i_ready, m2_ready = sem("consts"), sem("masks_done"), sem("m2i_ready"), sem("m2_ready")
        vec_ps, vec_done = sem("vec_ps"), sem("vec_done")
        n_sq, n_rt, n_xn, n_tp, n_evA, n_evD = (sem(n) for n in ("n_sq", "n_rt", "n_xn", "n_tp", "n_evA", "n_evD"))
        qk_ps, sq_done, ssq_ps, rt_done, rr_done, qk_done = (sem(n) for n in ("qk_ps", "sq_done", "ssq_ps", "rt_done", "rr_done", "qk_done"))
        v_ps, v_ev = sem("v_ps"), sem("v_ev")
        s_ps, sm_done, nm_done, p_done, t_ps, pt_done, pv_done, o_ev = (sem(n) for n in ("s_ps", "sm_done", "nm_done", "p_done", "t_ps", "pt_done", "pv_done", "o_ev"))
        r_ps, rowd, rowexp, coef_done, bc_ps, bc_done = (sem(n) for n in ("r_ps", "rowd", "rowexp", "coef_done", "bc_ps", "bc_done"))
        oT_done, oT_high, oT_low = sem("oT_done"), sem("oT_high"), sem("oT_low")
        wo_ps, x1_done = sem("wo_ps"), sem("x1_done")
        f_ps, f_id, conv_done, silu_done, act_done = (sem(n) for n in ("f_ps", "f_id", "conv_done", "silu_done", "act_done"))
        dn_ps, x2_done = sem("dn_ps"), sem("x2_done")
        pj_ps, pjA, pjD = sem("pj_ps"), sem("pjA"), sem("pjD")
        dist_done, al_done, wal_done = sem("dist_done"), sem("al_done"), sem("wal_done")
        sd_ps, sd_done, dnm_done, de_done, a_done, dt_ps, dpt_done, dpv, dO_ev = (sem(n) for n in ("sd_ps", "sd_done", "dnm_done", "de_done", "a_done", "dt_ps", "dpt_done", "dpv", "dO_ev"))
        lam_sum, lam_exp, lam_done = sem("lam_sum"), sem("lam_exp"), sem("lam_done")
        on_sq, on_ps, on_rt, on_rr, on_done = (sem(n) for n in ("on_sq", "on_ps", "on_rt", "on_rr", "on_done"))
        sw_ps, sw_done, wnm_done, we_done, aw_done, wt_ps, wpt_done, wpv, wO_ev = (sem(n) for n in ("sw_ps", "sw_done", "wnm_done", "we_done", "aw_done", "wt_ps", "wpt_done", "wpv", "wO_ev"))
        sx_ps, xnm_done, xe1_done, ax_done, xt_ps, xpt_done, xpv, xO_ev = (sem(n) for n in ("sx_ps", "xnm_done", "xe1_done", "ax_done", "xt_ps", "xpt_done", "xpv", "xO_ev"))
        g_ps, gsig, m_done, br_high, br_low = (sem(n) for n in ("gate_ps", "gate_sig", "m_done", "br_high", "br_low"))
        wo2_ps, x3_done = sem("wo2_ps"), sem("x3_done")
        h2_done, rt_ps, lg_done, lexp, affd, affT_ps, slot_d, slot_ps, oh_done, ohg_done, og_ps, og_ev = (sem(n) for n in ("h2_done", "rt_ps", "lg_done", "lexp", "affd", "affT_ps", "slot_d", "slot_ps", "oh_done", "ohg_done", "og_ps", "og_ev"))
        ohgD_done = sem("ohgD_done")
        ga_ps, b67_free, sg_done, ae_done, ye_done, st_done, c_ps = (sem(n) for n in ("ga_ps", "b67_free", "sg_done", "ae_done", "ye_done", "st_done", "c_ps"))
        f_sq, f_rt, o_done, out_done = sem("f_sq"), sem("f_rt"), sem("o_done"), sem("out_done")

        PJ = "A" * 8 + "D" * 8 + "ADAD" * 2
        PJ_WA = len(PJ)
        PJ += "A" * 8 + "DD" + "AAAA"
        PJ_XA = len(PJ)
        PJ += "D" * 8 + "DDDD" + "A" * 8

        def pj_bank_free(eng, n):
            if n >= 4:
                m = n - 4
                eng.wait_ge(pjA if PJ[m] == "A" else pjD, PJ[:m + 1].count(PJ[m]))

        def pj_all_done(eng, n):
            eng.wait_ge(pjA, PJ[:n].count("A"))
            eng.wait_ge(pjD, PJ[:n].count("D"))

        def cols_all_k(w, c0, n):
            return w[:, c0:c0 + n].rearrange("(k p) n -> p k n", p=P)

        def rows_k(w, k0, nk, c0, n):
            return w[k0 * P:(k0 + nk) * P, c0:c0 + n].rearrange("(k p) n -> p k n", p=P)

        def col_chunks(w, c0, n):
            return [cols_all_k(w, c, 256) for c in range(c0, c0 + n, 256)]

        def tok_chunks(w, c0, n, nk=KT):
            return [rows_k(w, k, 4, c, 512) for c in range(c0, c0 + n, 512) for k in range(0, nk, 4)]

        chunks, halves, stage = [], [], {}
        used = [0]

        def cols_half(i):
            return lambda slot: slot.rearrange("p (k n) -> p k n", k=KT)[:, :, i * P:(i + 1) * P]

        def rows_half(i):
            return lambda slot: slot[:, i * HALF:(i + 1) * HALF].rearrange("p (k n) -> p k n", k=1)

        def w_used_next():
            used[0] += 1
            return w_used, used[0]

        def split_cols(srcs, done, value):
            for i, src in enumerate(srcs):
                for half in range(2):
                    halves.append((len(chunks), cols_half(half), done, value + 2 * i + half + 1))
                chunks.append(src)

        def split_rows(srcs, done, value):
            for i, src in enumerate(srcs):
                for half in range(2):
                    d, v = (done, value) if (i, half) == (len(srcs) - 1, 1) else w_used_next()
                    halves.append((len(chunks), rows_half(half), d, v))
                chunks.append(src)

        w1, wi, wm = I["attn_w_in"][0], I["w_in_2"][0], I["w_mem_kv_2"][0]
        for g in range(GROUPS):
            b = 3 * g * GW
            split_cols(col_chunks(w1, b, 2 * GW), qk_ps, 8 * g)
            split_rows(tok_chunks(w1, b + 2 * GW, GW), v_ps, TT * (g + 1))
        for half in range(2):
            split_rows(tok_chunks(I["attn_w_out"][0], half * 512, 512, GW // P), wo_ps, 4 * (half + 1))
        for jj in range(FB // 2):
            for i in range(2):
                for j in range(2):
                    halves.append((len(chunks) + j, cols_half(i), f_ps, 4 * jj + 2 * i + j + 1))
            for c in (0, FH):
                chunks += col_chunks(I["ffn_w_up"][0], c + 256 * jj, 256)
        split_rows([rows_k(I["ffn_w_down"][0], f, 2, 0, D) for f in range(0, FB, 2)], dn_ps, 8)
        stage["da"] = len(halves)
        split_cols(col_chunks(wi, COL["daq"], 2048), pj_ps, 0)
        for half in range(2):
            split_rows(tok_chunks(wi, COL["dav"] + 512 * half, 512), pj_ps, 20 + 4 * half)
        stage["wa"] = len(halves)
        split_cols(col_chunks(wi, COL["waq"], 1280), pj_ps, PJ_WA)
        split_rows(col_chunks(wi, COL["wav"], 256), pj_ps, PJ_WA + 14)
        stage["xa"] = len(halves)
        split_cols(col_chunks(wm, 0, D), pj_ps, PJ_XA)
        for half in range(2):
            split_rows(tok_chunks(wm, D + 512 * half, 512), pj_ps, PJ_XA + 10 + 2 * half)
        stage["xq"] = len(halves)
        split_cols(col_chunks(wi, COL["xaq"], 1024), pj_ps, PJ_XA + 12)
        wb = [I["w_da_o_2"][0], I["w_wa_o_2"][0], I["w_xa_o_2"][0]]
        for b in range(NB):
            for jj in range(4):
                split_cols(col_chunks(wi, COL["gate"] + b * D + jj * 256, 256), g_ps, 16 * b + 4 * jj)
                split_cols(col_chunks(wb[b], jj * 256, 256), g_ps, 16 * b + 4 * jj + 2)
        for half in range(2):
            split_rows(tok_chunks(I["w_out_2"][0], 512 * half, 512), wo2_ps, 4 * (half + 1))
        NCH, NH = len(chunks), len(halves)
        split_end = [max(n + 1 for n, h in enumerate(halves) if h[0] == c) for c in range(NCH)]
        before = [len(range(i, NCH, RS)) if i < RS else 0 for i in range(NS)]
        by_act = range(stage["xa"] + 2, stage["xq"])
        SEQ = 14
        ECH = 48
        wg_e, wu_e, wd_e = (I[n].rearrange("l e a b -> (l e a b)")
                            for n in ("w_exp_gate_2", "w_exp_up_2", "w_exp_down_2"))

        units = []
        for g in range(GROUPS):
            for h in range(HEADS1):
                units += [(g, h, [0, 1]), (g, h, [2, 3])] if g == 0 else [(g, h, [0, 1, 2, 3])]
        UB = [0, 16, 24, 32]
        head_end = {}
        for n, (g, h, _) in enumerate(units):
            head_end[(g, h)] = n + 1
        nbase = [sum(NORM_TILES[:k]) for k in range(6)]

        block = ctx.enter_context(nc.Block())

        @block.sync
        def _(sp):
            for c, src in enumerate(chunks):
                if c == 0:
                    sp.wait_ge(in_x[0], 16)
                if c == 1:
                    sp.wait_ge(in_vec, 16 * 13)
                if c >= RS:
                    sp.wait_ge(w_split, split_end[c - RS])
                dst = ring[:, c % RS, :].rearrange("p (k n) -> p k n", k=src.shape[1])
                sp.dma_start(dst, src).then_inc(landed[c % RS], 16)

            def expert_chunk(at, c, free=None):
                a, i = c // 24, c % 24
                s = c % NS
                if i < 16:
                    w, k, dst = (wg_e, wu_e)[i % 2], i // 2, ring[:, s, :]
                else:
                    w, k, dst = wd_e, i - 16, ring[:, s, :].rearrange("p (j n) -> p j n", j=2)
                at = at + (8 * a + k) * P * SLOT
                if free is not None:
                    sp.wait_ge(e_chunks, free)
                src = w[bass.ds(at, P * SLOT)]
                if i < 16:
                    src = src.rearrange("(p n) -> p n", p=P)
                else:
                    src = src.rearrange("(j p n) -> p j n", p=P, j=2)
                sp.dma_start(dst, src).then_inc(landed[s], 16)

            PAIR_W = 2 * D * FE
            sp.wait_ge(w_split, NH)
            for c in range(NS):
                if c == RS:
                    sp.wait_ge(wo2_ps, 8)
                expert_chunk(0, c)
            with sp.Fori(0, PAIRS - 1) as q:
                for c in range(ECH):
                    n = c + NS
                    free = None if n == 16 else q * ECH + (c + (2 if n == 15 else 1))
                    expert_chunk(q * PAIR_W + n // ECH * PAIR_W, n % ECH, free)
            for c in range(ECH - NS):
                sp.wait_ge(e_chunks, (PAIRS - 1) * ECH + c + 1)
                expert_chunk((PAIRS - 1) * PAIR_W, c + NS)
            for t in range(TT):
                sp.wait_ge(o_done, t + 1)
                sp.dma_start(out[0, t * P:(t + 1) * P, :], xn2[:, t, :]).then_inc(out_done, 16)
            sp.wait_ge(out_done, 16 * TT)

        @block.gpsimd
        def _(pool):
            n = [0]

            def link(ins):
                n[0] += 1
                ins.then_inc(pool_c, 1)
                pool.wait_ge(pool_c, n[0])

            at = [0]

            def split(n):
                for i in range(at[0], n):
                    c, view, _, _ = halves[i]
                    if i == 0 or halves[i - 1][0] < c:
                        pool.wait_ge(landed[c % RS], 16 * (c // RS + 1))
                    if i >= 2:
                        pool.wait_ge(halves[i - 2][2], halves[i - 2][3])
                    by_pool = i + 1 - len(range(by_act.start, min(i + 1, by_act.stop)))
                    w = view(ring[:, c % RS, :])
                    hi, lo = (v[:, i % 2, :].rearrange("p (k n) -> p k n", k=w.shape[1]) for v in (w_hi, w_lo))
                    if i in by_act:
                        pool.wait_ge(w_highA, i + 1 - by_act.start)
                    else:
                        nc.gpsimd.tensor_tensor(hi, w, one[:].unsqueeze(2).to_broadcast(list(w.shape)),
                                                ALU.mult).then_inc(w_high, 1)
                        pool.wait_ge(w_high, by_pool)
                    nc.gpsimd.tensor_tensor(lo, w, hi.bitcast(f32), ALU.subtract).then_inc(w_split, 1)
                at[0] = n

            nc.gpsimd.memset(one[:], 1.0)
            nc.gpsimd.memset(ident[:], 0.0)
            nc.gpsimd.memset(mean64[:], 0.0)
            nc.gpsimd.memset(epsb[:], EPS)
            nc.gpsimd.memset(mean128[:], 1.0 / 128)
            link(nc.gpsimd.memset(mask[:], 0.0))
            link(nc.gpsimd.memset(selB[:], 0.0))
            nc.gpsimd.memset(mean64[0:64, 0:64], 1.0 / 64)
            link(nc.gpsimd.memset(mean64[64:128, 64:128], 1.0 / 64))
            nc.gpsimd.affine_select(out=ident[:], in_=ident[:], compare_op=ALU.not_equal, fill=1.0, base=0,
                                    pattern=[[-1, P]], channel_multiplier=1).then_inc(consts, 1)
            nc.gpsimd.iota(m2i.rearrange("p (c k) -> p c k", c=4), pattern=[[0, 4], [-1, P]], base=P,
                           channel_multiplier=1).then_inc(m2i_ready, 1)
            split(2)
            s4 = selB[0:HEADS1].rearrange("p b (a c) -> p b a c", a=2)
            nc.gpsimd.affine_select(out=s4, in_=s4, compare_op=ALU.not_equal, fill=1.0, base=0,
                                    pattern=[[-2, 4], [-1, 2], [0, 64]], channel_multiplier=1)

            def causal(v, nt):
                return nc.gpsimd.affine_select(out=v, in_=v, compare_op=ALU.is_ge, fill=NEG, base=0,
                                               pattern=[[0, nt], [-1, P]], channel_multiplier=1)

            m0 = mask[:, 0:2, :].rearrange("p a (t s k) -> p (a t) s k", t=2, s=2)
            causal(m0[:, :, 1, :], 4)
            pv = m0[:, :, 0, :]
            link(nc.gpsimd.affine_select(out=pv, in_=pv, compare_op=ALU.is_ge, fill=NEG, base=0,
                                         pattern=[[0, 4], [1, P]], channel_multiplier=-1))
            nc.gpsimd.memset(m0[:, 0, 0, :], NEG)
            causal(mask[:, 2, :].rearrange("p (c k) -> p c k", c=4), 4)
            pool.wait_ge(m2_ready, 1)
            causal(mask[:, 3, :].rearrange("p (c k) -> p c k", c=4), 4).then_inc(masks_done, 1)

            split(stage["da"] + 2)
            pool.wait_ge(x2_done, 8)
            pool.wait_ge(n_xn, nbase[3])
            link(nc.gpsimd.iota(dist, pattern=[[-1, 896]], base=384, channel_multiplier=1,
                                allow_small_or_imprecise_dtypes=True))
            link(nc.gpsimd.tensor_scalar(alibi[:, 0, :], dist, 0.0, 2.0, ALU.max, ALU.mult))
            link(nc.gpsimd.tensor_tensor(dist, alibi[:, 0, :], dist, ALU.subtract))
            for h in range(DA_H):
                if h == 2:
                    split(stage["wa"] + 2)
                if h >= 2:
                    pool.wait_ge(sd_done, 8 * (h - 1))
                nc.gpsimd.tensor_scalar(alibi[:, h % 2, :], dist, -(2.0 ** (-8.0 * (h + 1) / DA_H)), None,
                                        ALU.mult).then_inc(al_done, 1)
            pool.wait_ge(sd_done, 64)
            link(nc.gpsimd.iota(wdist, pattern=[[-1, 384]], base=P, channel_multiplier=1,
                                allow_small_or_imprecise_dtypes=True))
            link(nc.gpsimd.tensor_scalar(walibi[:, 0, :], wdist, 0.0, 2.0, ALU.max, ALU.mult))
            link(nc.gpsimd.tensor_tensor(wdist, walibi[:, 0, :], wdist, ALU.subtract))
            link(nc.gpsimd.affine_select(out=wdist, in_=wdist, compare_op=ALU.is_ge, fill=-NEG, base=0,
                                         pattern=[[1, 384]], channel_multiplier=-1))
            link(nc.gpsimd.affine_select(out=wdist, in_=wdist, compare_op=ALU.is_ge, fill=-NEG, base=256,
                                         pattern=[[-1, 384]], channel_multiplier=1))
            for h in range(WA_H):
                if h == 2:
                    split(stage["xa"] + 2)
                if h >= 2:
                    pool.wait_ge(sw_done, 4 * (h - 1))
                nc.gpsimd.tensor_scalar(walibi[:, h % 2, :], wdist, -(2.0 ** (-8.0 * (h + 1) / WA_H)), None,
                                        ALU.mult).then_inc(wal_done, 1)

            split(NH)
            pool.wait_ge(x3_done, 8)
            nc.gpsimd.iota(iota1, pattern=[[1, CAP]], base=1, channel_multiplier=0,
                           allow_small_or_imprecise_dtypes=True)
            nc.gpsimd.memset(ones, 1.0).then_inc(slots_ready, 1)
            for t in range(2):
                pool.wait_ge(oh_done, t + 1)
                nc.gpsimd.tensor_tensor(OHg[:, t, :].rearrange("p (e c) -> p e c", e=NE),
                                        OH[:, t, :].rearrange("p (e c) -> p e c", e=NE),
                                        aff[:, t, :].unsqueeze(2).to_broadcast([P, NE, CAP]),
                                        ALU.mult).then_inc(ohg_done, 1)

        @block.scalar
        def _(act):
            A = nc.scalar.activation
            F = ACT
            for t in range(TT):
                act.dma_start(x[:, t, :], I["x"][0, t * P:(t + 1) * P, :]).then_inc(in_x[t], 16)
            for i, n in enumerate(("mixer_norm", "ffn_norm", "attn_norm_g_2", "mem_norm_g_2", "ffn_norm_g_2")):
                act.dma_start(vrow[8 * i:8 * i + 8, 0, :],
                              I[n][0].rearrange("(k p) -> k p", p=P)).then_inc(in_vec, 16)
            act.dma_start(vrow[CB:CB + 44, 0, :], I["ffn_conv_b"][0].rearrange("(k p) -> k p", p=P)).then_inc(in_vec, 16)
            act.dma_start(vrow[0:88, 1, :], I["ffn_conv_w"][0, 0:2].rearrange("a (k p) -> (a k) p", p=P)).then_inc(in_vec, 16)
            act.dma_start(vrow[0:44, 2, :], I["ffn_conv_w"][0, 2].rearrange("(k p) -> k p", p=P)).then_inc(in_vec, 16)
            for half in range(2):
                c = slice(64 * half, 64 * half + 64)
                act.dma_start(vrow[0:3, 3, c], I["attn_q_gain"][0]).then_inc(in_vec, 16)
                act.dma_start(vrow[3:6, 3, c], I["attn_k_gain"][0]).then_inc(in_vec, 16)
            act.dma_start(vrow[6:7, 3, :], I["da_subln_g_2"]).then_inc(in_vec, 16)
            act.dma_start(wr[:], I["w_router_2"][0].rearrange("(k p) e -> p k e", p=P)).then_inc(in_small, 16)
            act.dma_start(sink[:], I["wa_sink_2"].partition_broadcast(P).rearrange("p a h -> p (a h)")).then_inc(in_small, 16)

            def norm(k, src, xbuf, ready=None):
                if k:
                    act.wait_ge(n_xn, nbase[k])
                for t in range(NORM_TILES[k]):
                    if ready is not None:
                        act.wait_ge(*ready(t))
                    if t:
                        act.wait_ge(n_sq, nbase[k] + t)
                    A(xbuf, src[:, t, :], F.Square, accum_out=ssq[:, t:t + 1]).then_inc(n_sq, 1)
                    act.wait_ge(n_sq, nbase[k] + t + 1)
                    A(ssq[:, t:t + 1], ssq[:, t:t + 1], F.Sqrt, bias=epsb[:], scale=1.0 / D).then_inc(n_rt, 1)

            def norm_hi(k, dst, gain, ntok):
                for kb in range(KT):
                    act.wait_ge(n_tp, 8 * k + kb + 1)
                    if kb == 0 and k:
                        act.wait_ge(n_evD, 8 * k)
                    A(dst[:, kb, :], ps[:, kb % 4, 0:ntok], F.Copy, scale=vec[:, gain + kb:gain + kb + 1]).then_inc(n_evA, 1)

            def norm_out(k, dst, gain, ntok):
                for kb in range(0, KT, 2):
                    act.wait_ge(n_tp, 8 * k + kb + 1)
                    A(dst[:, kb, :], ps[:, kb % 4, 0:ntok], F.Copy, scale=vec[:, gain + kb:gain + kb + 1]).then_inc(n_evA, 1)

            act.wait_ge(consts, 1)
            norm(0, x, junk, lambda t: (in_x[t], 16))
            act.wait_ge(vec_done, 1)
            norm_hi(0, h_hi, MIXG, S)

            for g in range(GROUPS):
                for b in range(9):
                    n = 8 * g + b
                    if b < 8:
                        act.wait_ge(qk_ps, n + 1)
                        if n >= 2:
                            act.wait_ge(ssq_ps, n - 1)
                        A(sq[:, n % 2, :], ps[:, n % 4, :], F.Square).then_inc(sq_done, 1)
                    if b:
                        m = n - 1
                        act.wait_ge(ssq_ps, m + 1)
                        if m >= 2:
                            act.wait_ge(rr_done, m - 1)
                        A(rt[:, m % 2, :], ps[:, 6 + m % 2, :], F.Sqrt, bias=epsb[:]).then_inc(rt_done, 1)
                for t in range(TT):
                    act.wait_ge(v_ps, TT * g + t + 1)
                    A(v1[:, t, :], ps[:, 4 + t, :], F.Copy).then_inc(v_ev, 1)
                for u in range(UB[g], UB[g + 1] + 2):
                    if u < UB[g + 1]:
                        _, h, tiles = units[u]
                        w = 512 // len(tiles)
                        act.wait_ge(nm_done, u + 1)
                        for i, t in enumerate(tiles):
                            last = A(sm[:, u % 3, i * w:(i + 1) * w], sm[:, u % 3, i * w:(i + 1) * w], F.Exp,
                                     bias=nm1[:, g, t, h:h + 1], accum_out=l1[:, g, t, h:h + 1])
                        last.then_inc(p_done, 1)
                    m = u - 2
                    if m >= UB[g] and head_end[units[m][0:2]] == m + 1:
                        h = units[m][1]
                        act.wait_ge(pv_done, m + 1)
                        r = slice(64 * (h % 2), 64 * (h % 2) + 64)
                        o, i_ = U[r, g, h // 2, :], ps[r, 2 + h % 2, :]
                        if g:
                            o = o.rearrange("p (j c) -> p c j", c=4)
                            i_ = i_.rearrange("p (c j) -> p c j", c=4)
                        A(o, i_, F.Copy).then_inc(o_ev, 1)
            act.wait_ge(rowd, 1)
            A(coef, coef, F.Exp).then_inc(rowexp, 1)

            for b in range(4):
                act.wait_ge(oT_done, b + 1)
                A(oT_hi[:, b, :], oT[:, b, :], F.Copy).then_inc(oT_high, 1)

            norm(1, x, junk, lambda t: (x1_done, TT + t + 1))
            norm_hi(1, h_hi, FFNG, S)
            for j in range(FB + 1):
                if j < FB:
                    for i, buf in enumerate((cg, cu)):
                        act.wait_ge(f_ps, 2 * j + i + 1)
                        if j >= 2:
                            act.wait_ge(act_done, j - 1)
                        A(buf[:, j % 2, :], ps[:, 2 * (j % 2) + i, :], F.Identity,
                          bias=vec[:, CB + 22 * i + j:CB + 22 * i + j + 1],
                          scale=vec[:, CW + 88 + 22 * i + j:CW + 88 + 22 * i + j + 1]).then_inc(f_id, 1)
                if j:
                    act.wait_ge(conv_done, 4 * (j - 1) + 3)
                    A(cg[:, (j - 1) % 2, :], cg[:, (j - 1) % 2, :], F.Silu).then_inc(silu_done, 1)

            norm(2, x, junk2, lambda t: (x2_done, 2 * t + 2))
            norm_hi(2, h_hi, ATTG, S)
            for i, n in enumerate(("da_lambda_q1_2", "da_lambda_k1_2", "da_lambda_q2_2", "da_lambda_k2_2")):
                act.dma_start(lamv[:, i, :], I[n].partition_broadcast(P).rearrange("p a d -> p (a d)")).then_inc(in_small, 16)
            for n in range(8):
                act.wait_ge(pj_ps, n + 1)
                A(da_q[:, n, :], ps[:, n % 4, :], F.Copy, scale=0.125).then_inc(pjA, 1)
            for n in range(16, 24):
                if PJ[n] == "A":
                    t, half = (n - 16) % 4, (n - 16) // 4
                    act.wait_ge(pj_ps, n + 1)
                    A(da_v[:, t, half * 512:half * 512 + 512], ps[:, n % 4, :], F.Copy).then_inc(pjA, 1)
            act.wait_ge(lam_sum, 1)
            A(lamsc[:, 0:2], lamsc[:, 0:2], F.Exp).then_inc(lam_exp, 1)

            def da_copy(u):
                h = u // 2
                for i in range(2):
                    qb = 2 * (u % 2) + i
                    act.wait_ge(dt_ps, 2 * u + i + 1)
                    if h >= 2:
                        act.wait_ge(dpv, h - 1)
                    A(da_pt[:, 4 * (h % 2):4 * (h % 2) + 4, qb * P:(qb + 1) * P],
                      ps[:, i, :].rearrange("p (k q) -> p k q", k=4), F.Copy).then_inc(dpt_done, 1)

            def da_out(h):
                act.wait_ge(dpv, h + 1)
                A(o_raw[:, h, :], ps[:, 2 + h % 2, :], F.Copy).then_inc(dO_ev, 1)

            for u in range(16 + 3):
                if u < 16:
                    act.wait_ge(dnm_done, u + 1)
                    for i in range(4):
                        last = A(da_e[:, u % 2, i, :], da_e[:, u % 2, i, :], F.Exp, bias=nmx[:, u % 2, i:i + 1],
                                 accum_out=lsum[:, u % 2, i:i + 1])
                    last.then_inc(de_done, 1)
                if 1 <= u <= 16:
                    da_copy(u - 1)
                if u >= 4 and u % 2 == 0:
                    da_out(u // 2 - 2)
            act.wait_ge(dpv, 8)
            act.dma_start(memt, I["mem_2"][0].rearrange("(t p) d -> p t d", p=P)).then_inc(in_mem, 16)
            for h in range(9):
                if h < 8:
                    act.wait_ge(dO_ev, h + 1)
                    if h >= 2:
                        act.wait_ge(on_ps, h - 1)
                    A(da_e[:, 0, h % 2, :], o_raw[:, h, :], F.Square).then_inc(on_sq, 1)
                if h:
                    m = h - 1
                    act.wait_ge(on_ps, m + 1)
                    if m >= 2:
                        act.wait_ge(on_rr, m - 1)
                    A(da_e[:, 0, 2 + m % 2, :], ps[:, 4 + m % 2, :], F.Sqrt, bias=epsb[:]).then_inc(on_rt, 1)
                    A(wa_q[:, m, :], ps[:, (PJ_WA + m) % 4, :], F.Copy, scale=0.125).then_inc(pjA, 1)

            for n in range(PJ_WA + 10, PJ_XA):
                act.wait_ge(pj_ps, n + 1)
                act.wait_ge(on_done, 8)
                A(wa_v[:, n - PJ_WA - 10, :], ps[:, n % 4, 0:256], F.Copy).then_inc(pjA, 1)

            def wa_copy(h):
                for i, nb in enumerate((4, 4, 2)):
                    m = 3 * h + i
                    act.wait_ge(wt_ps, m + 1)
                    if h >= 2:
                        act.wait_ge(wpv, h - 1)
                    b0 = 10 * (h % 2) + 4 * i
                    A(wa_pt[:, b0:b0 + nb, :], ps[:, i, 0:nb * P].rearrange("p (b q) -> p b q", b=nb),
                      F.Copy).then_inc(wpt_done, 1)

            def wa_out(h):
                act.wait_ge(wpv, h + 1)
                r = slice(64 * (h % 2), 64 * (h % 2) + 64)
                A(o_wa[r, h // 2, :], ps[r, 3, :], F.Copy).then_inc(wO_ev, 1)

            act.wait_ge(in_small, 96)
            for u in range(WA_H + 2):
                if u < WA_H:
                    act.wait_ge(wnm_done, u + 1)
                    for qb in range(4):
                        c0, c1 = (P if qb == 0 else 0), (256 if qb == 3 else 384)
                        v = wa_p[:, u % 2, qb, c0:c1]
                        A(v, v, F.Exp, bias=nmx[:, u % 2, qb:qb + 1], accum_out=lsum[:, u % 2, qb:qb + 1])
                    A(esink[:, u % 2, :], nmx[:, u % 2, :], F.Exp, bias=sink[:, u:u + 1]).then_inc(we_done, 1)
                if 1 <= u <= WA_H:
                    wa_copy(u - 1)
                if u >= 2:
                    wa_out(u - 2)

            act.wait_ge(in_mem, 16)
            norm(3, memt, junk[:, :])
            norm_hi(3, mem_hi, MEMG, MEM)
            for i in by_act:
                c, view, _, _ = halves[i]
                act.wait_ge(landed[c % RS], 16 * (c // RS + 1))
                act.wait_ge(halves[i - 2][2], halves[i - 2][3])
                w = view(ring[:, c % RS, :])
                A(w_hi[:, i % 2, :].rearrange("p (k n) -> p k n", k=w.shape[1]), w, F.Copy).then_inc(w_highA, 1)
            for n in range(PJ_XA + 12, PJ_XA + 20):
                act.wait_ge(pj_ps, n + 1)
                A(xa_q[:, n - PJ_XA - 12, :], ps[:, n % 4, :], F.Copy, scale=0.0625).then_inc(pjA, 1)
            for u in range(XA_H + 1):
                if u < XA_H:
                    if u >= 2:
                        act.wait_ge(xt_ps, 2 * (u - 1))
                    for qb in range(4):
                        act.wait_ge(xnm_done, 4 * u + qb + 1)
                        A(xa_p[:, u % 2, qb, :], ps[:, 4 + qb, 0:MEM], F.Exp, bias=nmx[:, u % 2, qb:qb + 1],
                          accum_out=lsum[:, u % 2, qb:qb + 1]).then_inc(xe1_done, 1)
                if u:
                    h = u - 1
                    for kb in range(2):
                        act.wait_ge(xt_ps, 2 * h + kb + 1)
                        if h >= 2:
                            act.wait_ge(xpv, 2 * (h - 1))
                        A(xa_pt[:, 2 * (h % 2) + kb, :], ps[:, kb, :], F.Copy).then_inc(xpt_done, 1)

            for n in range(NB * KT):
                if n % KT == 0:
                    act.wait_ge(on_done, 8)
                    act.wait_ge(xO_ev, 8)
                    if n:
                        act.wait_ge(g_ps, 2 * n)
                        act.wait_ge(br_low, n)
                    for k in range(KT):
                        A(br_hi[:, k, :], (o_da, o_wa, o_xa)[n // KT][:, k, :], F.Copy).then_inc(br_high, 1)
                act.wait_ge(g_ps, 4 * (n // 2) + n % 2 + 1)
                if n >= 2:
                    act.wait_ge(m_done, n - 1)
                A(sg[:, n % 2, :], ps[:, 2 * (n % 4), :], F.Sigmoid).then_inc(gsig, 1)

            act.wait_ge(x3_done, 1)
            act.dma_start(h2g, I["ffn_norm_g_2"].partition_broadcast(P).rearrange("p a d -> p (a d)")).then_inc(in_moe, 16)
            act.dma_start(fing, I["final_norm_g_2"].partition_broadcast(P)).then_inc(in_moe, 16)
            norm(4, x, junk, lambda t: (x3_done, TT + t + 1))
            norm_out(4, hT, FFN2G, S)
            act.wait_ge(lg_done, 1)
            A(lg, lg, F.Exp).then_inc(lexp, 1)
            with act.Fori(0, PAIRS) as q:
                for a in range(2):
                    act.wait_ge(e_chunks, q * ECH + (24 * a + 16))
                    for i in range(2):
                        act.wait_ge(ae_done, q * 4 + (2 * a + i + 1))
                        A(sg_e[64:128, i * 1024:i * 1024 + 1024],
                          ps[0:CAP, 2 * i:2 * i + 2, :].rearrange("p b n -> p (b n)"), F.Silu).then_inc(sg_done, 1)
            for t in range(TT):
                act.wait_ge(b67_free, (PAIRS - 1) * SEQ + (10 + 2 * t))
                if t:
                    act.wait_ge(f_sq, t)
                A(junk, x[:, t, :], F.Square, accum_out=ssq[:, t:t + 1]).then_inc(f_sq, 1)
                act.wait_ge(f_sq, t + 1)
                A(ssq[:, t:t + 1], ssq[:, t:t + 1], F.Sqrt, bias=epsb[:], scale=1.0 / D).then_inc(f_rt, 1)

        @block.vector
        def _(dve):
            V = nc.vector
            n_ = [0]

            def link(ins):
                n_[0] += 1
                ins.then_inc(dve_c, 1)
                dve.wait_ge(dve_c, n_[0])

            dve.wait_ge(m2i_ready, 1)
            link(V.tensor_scalar(m2i, m2i, 3, None, ALU.bitwise_and))
            V.tensor_scalar(mask[:, 3, :], m2i, 0.0, NEG, ALU.is_gt, ALU.mult).then_inc(m2_ready, 1)

            def norm(k, src, dst):
                for t in range(NORM_TILES[k]):
                    dve.wait_ge(n_rt, nbase[k] + t + 1)
                    link(V.reciprocal(rstd[:, t:t + 1], ssq[:, t:t + 1]))
                    V.tensor_scalar(dst[:, t, :], src[:, t, :], rstd[:, t:t + 1], None, ALU.mult).then_inc(n_xn, 1)

            def norm_lo(k, dst, high, gain, ntok):
                for kb in range(KT):
                    dve.wait_ge(n_evA, 8 * k + kb + 1)
                    V.scalar_tensor_tensor(out=dst[:, kb, :], in0=ps[:, kb % 4, 0:ntok],
                                           scalar=vec[:, gain + kb:gain + kb + 1], in1=high[:, kb, :].bitcast(f32),
                                           op0=ALU.mult, op1=ALU.subtract).then_inc(n_evD, 1)

            def norm_out(k, dst, gain, ntok):
                for kb in range(1, KT, 2):
                    dve.wait_ge(n_tp, 8 * k + kb + 1)
                    V.tensor_scalar(dst[:, kb, :], ps[:, kb % 4, 0:ntok], vec[:, gain + kb:gain + kb + 1], None,
                                    ALU.mult).then_inc(n_evD, 1)

            norm(0, x, xn)
            dve.wait_ge(vec_ps, 1)
            link(V.tensor_copy(vec[:], ps[:, 7, 0:NVEC]))
            V.tensor_scalar(vec[:, QG:QG + 3], vec[:, QG:QG + 3], DH ** -0.5, None, ALU.mult)
            V.tensor_scalar(vec[:, SUBG:SUBG + 1], vec[:, SUBG:SUBG + 1], 0.8, None, ALU.mult).then_inc(vec_done, 1)
            dve.wait_ge(vec_done, 1)
            norm_lo(0, h_lo, h_hi, MIXG, S)

            V.memset(qk[64:128, 4:8, :], 0.0)
            V.memset(k1_odd[0:64], 0.0)
            dve.wait_ge(masks_done, 1)
            for g in range(GROUPS):
                for b in range(8):
                    n = 8 * g + b
                    gain = (QG if b < 4 else KG) + g
                    dve.wait_ge(rt_done, n + 1)
                    V.reciprocal(rr[:, n % 2, :], rt[:, n % 2, :]).then_inc(rr_done, 1)
                    dve.wait_ge(rr_done, n + 1)
                    o, a, r = qk[:, b, :], ps[:, n % 4, :], rr[:, n % 2, :]
                    if g:
                        o = o.rearrange("p (c j) -> p j c", c=4)
                        a, r = (v.rearrange("p (j c) -> p j c", c=4) for v in (a, r))
                    if b < 4:
                        parts = [(o, slice(0, P))]
                    else:
                        odd = k1_odd[:, b - 4, :]
                        parts = [(o, slice(0, 64)), (odd.rearrange("p (c j) -> p j c", c=4) if g else odd, slice(64, P))]
                    for o, p in parts:
                        last = V.scalar_tensor_tensor(out=o[p], in0=a[p], scalar=vec[p, gain:gain + 1], in1=r[p],
                                                      op0=ALU.mult, op1=ALU.mult)
                    last.then_inc(qk_done, 1)
                for u in range(UB[g], UB[g + 1] + 1):
                    if u < UB[g + 1]:
                        _, h, tiles = units[u]
                        nt = len(tiles)
                        mrow = (0 if tiles[0] == 0 else 1) if g == 0 else g + 1
                        dve.wait_ge(s_ps, u + 1)
                        if u >= 3:
                            dve.wait_ge(t_ps, u - 2)
                        V.tensor_tensor(sm[:, u % 3, :], ps[:, 4 + u % 3, :], mask[:, mrow, :],
                                        ALU.add).then_inc(sm_done, 1)
                        dve.wait_ge(sm_done, u + 1)
                        V.tensor_reduce(nm1[:, g, tiles[0]:tiles[0] + nt, h],
                                        sm[:, u % 3, :].rearrange("p (t k) -> p t k", t=nt), AX.X, ALU.max,
                                        negate=True).then_inc(nm_done, 1)
                    m = u - 1
                    if m >= UB[g]:
                        dve.wait_ge(t_ps, m + 1)
                        if m >= 2:
                            dve.wait_ge(pv_done, m - 1)
                        V.tensor_copy(pt1[:, m % 2, :], ps[:, m % 2, :]).then_inc(pt_done, 1)
            dve.wait_ge(t_ps, UB[3])
            link(V.memset(coef_all, 0.0))
            for i in range(6):
                g = i % 3
                dve.wait_ge(r_ps, i + 1)
                o, a = rows[:, i, :], ps[0:HEADS1, i, :]
                if g:
                    o = o.rearrange("p (j c) -> p c j", c=4)
                    a = a.rearrange("p (c j) -> p c j", c=4)
                link(V.tensor_copy(o, a))
            dve.wait_ge(pv_done, UB[3])
            link(V.tensor_tensor(crow[:, 0, :], rows[:, 0, :], rows[:, 1, :], ALU.min))
            link(V.tensor_tensor(crow[:, 0, :], crow[:, 0, :], rows[:, 2, :], ALU.min))
            for g in range(GROUPS):
                last = V.tensor_tensor(coef[:, g, :], crow[:, 0, :], rows[:, g, :], ALU.subtract)
            last.then_inc(rowd, 1)
            dve.wait_ge(rowexp, 1)
            for g in range(GROUPS):
                last = V.tensor_tensor(rows[:, 3 + g, :], rows[:, 3 + g, :], coef[:, g, :], ALU.mult)
            link(last)
            link(V.tensor_tensor(crow[:, 0, :], rows[:, 3, :], rows[:, 4, :], ALU.add))
            link(V.tensor_tensor(crow[:, 0, :], crow[:, 0, :], rows[:, 5, :], ALU.add))
            link(V.reciprocal(crow[:, 1, :], crow[:, 0, :]))
            for g in range(GROUPS):
                last = V.tensor_tensor(coef[:, g, :], coef[:, g, :], crow[:, 1, :], ALU.mult)
            last.then_inc(coef_done, 1)
            dve.wait_ge(o_ev, 24)
            for n in range(12):
                b, g = n // 3, n % 3
                dve.wait_ge(bc_ps, n + 1)
                o = oT[:, b, :] if g == 0 else ctmp[:, n % 2, :]
                V.tensor_tensor(o, ps[:, 6 + n % 2, :], U[:, g, b, :], ALU.mult).then_inc(bc_done, 1)
                dve.wait_ge(bc_done, n + 1)
                if g:
                    link(V.tensor_tensor(oT[:, b, :], oT[:, b, :], ctmp[:, n % 2, :], ALU.add))
                if g == 2:
                    dve.sem_inc(oT_done, 1)
                if g == 2 and b:
                    dve.wait_ge(oT_high, b)
                    V.tensor_tensor(oT_lo[:, b - 1, :], oT[:, b - 1, :], oT_hi[:, b - 1, :].bitcast(f32),
                                    ALU.subtract).then_inc(oT_low, 1)
            dve.wait_ge(oT_high, 4)
            V.tensor_tensor(oT_lo[:, 3, :], oT[:, 3, :], oT_hi[:, 3, :].bitcast(f32), ALU.subtract).then_inc(oT_low, 1)

            def residual(sem_ps, sem_done, order, banks):
                for n, (half, t) in enumerate(order):
                    dve.wait_ge(sem_ps, n + 1)
                    xv = x[:, t, half * 512:half * 512 + 512]
                    V.tensor_tensor(xv, ps[:, banks(t, half), :], xv, ALU.add).then_inc(sem_done, 1)

            residual(wo_ps, x1_done, [(n // 4, n % 4) for n in range(8)], lambda t, half: 4 * half + t)

            norm(1, x, xn)
            norm_lo(1, h_lo, h_hi, FFNG, S)
            for j in range(FB + 1):
                if j < FB:
                    dve.wait_ge(f_id, 2 * j + 2)
                    cs = 4 * j
                    for k, sh in ((1, 1), (0, 2)):
                        for i, buf in enumerate((cg, cu)):
                            v = buf[:, j % 2, sh:]
                            if sh == 2:
                                dve.wait_ge(conv_done, cs + i + 1)
                            V.scalar_tensor_tensor(
                                out=v, in0=ps[:, 2 * (j % 2) + i, 0:S - sh],
                                scalar=vec[:, CW + 44 * k + 22 * i + j:CW + 44 * k + 22 * i + j + 1],
                                in1=v, op0=ALU.mult, op1=ALU.add).then_inc(conv_done, 1)
                if j:
                    m = j - 1
                    dve.wait_ge(silu_done, m + 1)
                    dve.wait_ge(conv_done, 4 * m + 4)
                    v = cg[:, m % 2, :]
                    link(V.tensor_tensor(v, v, cu[:, m % 2, :], ALU.mult))
                    link(V.tensor_copy(act_hi[:, m, :], v))
                    V.tensor_tensor(act_lo[:, m, :], v, act_hi[:, m, :].bitcast(f32), ALU.subtract).then_inc(act_done, 1)
            residual(dn_ps, x2_done, [(n % 2, n // 2) for n in range(8)], lambda t, half: 2 * t + half)

            norm(2, x, xn)
            norm_lo(2, h_lo, h_hi, ATTG, S)
            V.memset(da_k[64:128], 0.0)
            V.memset(da_k1[0:64], 0.0)
            for n in range(8, 24):
                if PJ[n] == "D":
                    dve.wait_ge(pj_ps, n + 1)
                    if n < 16:
                        V.tensor_copy(da_k[0:64, n - 8, :], ps[0:64, n % 4, :])
                        V.tensor_copy(da_k1[64:128, n - 8, :], ps[64:128, n % 4, :]).then_inc(pjD, 1)
                    else:
                        t, half = (n - 16) % 4, (n - 16) // 4
                        V.tensor_copy(da_v[:, t, half * 512:half * 512 + 512], ps[:, n % 4, :]).then_inc(pjD, 1)
            dve.wait_ge(in_small, 96)
            for i in range(2):
                last = V.tensor_tensor_reduce(out=lamv[:, 2 * i, :], in0=lamv[:, 2 * i, :], in1=lamv[:, 2 * i + 1, :],
                                              scale=1.0, scalar=0.0, op0=ALU.mult, op1=ALU.add,
                                              accum_out=lamsc[:, i:i + 1])
            last.then_inc(lam_sum, 1)
            dve.wait_ge(lam_exp, 1)
            link(V.tensor_tensor(lamsc[:, 2:3], lamsc[:, 1:2], lamsc[:, 0:1], ALU.subtract))
            link(V.tensor_scalar(lamsc[:, 3:4], lamsc[:, 2:3], -0.2, None, ALU.add))

            def da_probs(u):
                dve.wait_ge(de_done, u + 1)
                link(V.reciprocal(rl[:, u % 2, :], lsum[:, u % 2, :]))
                c1 = rl[:, u % 2, :].rearrange("p (q m) -> p q m", m=2)[:, :, 1]
                link(V.tensor_scalar(c1, c1, lamsc[:, 3:4], None, ALU.mult))
                for i in range(2):
                    e0, e1 = da_e[:, u % 2, 2 * i, :], da_e[:, u % 2, 2 * i + 1, :]
                    link(V.tensor_scalar(e0, e0, rl[:, u % 2, 2 * i:2 * i + 1], None, ALU.mult))
                    last = V.scalar_tensor_tensor(out=e0, in0=e1, scalar=rl[:, u % 2, 2 * i + 1:2 * i + 2], in1=e0,
                                                  op0=ALU.mult, op1=ALU.add)
                last.then_inc(a_done, 1)

            for u in range(17):
                if u == 16:
                    da_probs(u - 1)
                if u < 16:
                    h = u // 2
                    if u % 2 == 0:
                        dve.wait_ge(al_done, h + 1)
                    if u >= 2:
                        dve.wait_ge(dt_ps, 2 * (u - 1))
                    for i in range(4):
                        qb = 2 * (u % 2) + i // 2
                        if u and i == 3:
                            da_probs(u - 1)
                        dve.wait_ge(sd_ps, 4 * u + i + 1)
                        V.tensor_tensor_reduce(out=da_e[:, u % 2, i, :], in0=ps[:, 4 + i, :],
                                               in1=alibi[:, h % 2, 384 - P * qb:896 - P * qb], scale=1.0,
                                               scalar=-3e38, op0=ALU.add, op1=ALU.max,
                                               accum_out=mx[:, u % 2, i:i + 1]).then_inc(sd_done, 1)
                    dve.wait_ge(sd_done, 4 * u + 4)
                    V.tensor_scalar(nmx[:, u % 2, :], mx[:, u % 2, :], -1.0, None, ALU.mult).then_inc(dnm_done, 1)
            for h in range(8):
                dve.wait_ge(on_rt, h + 1)
                V.reciprocal(da_e[:, 1, h % 2, :], da_e[:, 0, 2 + h % 2, :]).then_inc(on_rr, 1)
                dve.wait_ge(on_rr, h + 1)
                V.scalar_tensor_tensor(out=o_da[:, h, :], in0=o_raw[:, h, :], scalar=vec[:, SUBG:SUBG + 1],
                                       in1=da_e[:, 1, h % 2, :], op0=ALU.mult, op1=ALU.mult).then_inc(on_done, 1)

            V.memset(wa_k[64:128], 0.0)
            V.memset(wa_k1[0:64], 0.0)
            for n in range(PJ_WA, PJ_XA):
                if PJ[n] == "D":
                    m = n - PJ_WA
                    dve.wait_ge(pj_ps, n + 1)
                    for i in range(2):
                        for o in range(2):
                            last = V.tensor_copy((wa_k, wa_k1)[o][64 * o:64 * o + 64, 2 * (m - 8) + i, :],
                                                 ps[64 * i:64 * i + 64, n % 4, :])
                    last.then_inc(pjD, 1)

            def wa_probs(h):
                dve.wait_ge(we_done, h + 1)
                link(V.tensor_tensor(lsum[:, h % 2, :], lsum[:, h % 2, :], esink[:, h % 2, :], ALU.add))
                link(V.reciprocal(rl[:, h % 2, :], lsum[:, h % 2, :]))
                for qb in range(4):
                    c0, c1 = (P if qb == 0 else 0), (256 if qb == 3 else 384)
                    v = wa_p[:, h % 2, qb, c0:c1]
                    last = V.tensor_scalar(v, v, rl[:, h % 2, qb:qb + 1], None, ALU.mult)
                last.then_inc(aw_done, 1)

            for u in range(WA_H + 1):
                if u == WA_H:
                    wa_probs(u - 1)
                if u < WA_H:
                    dve.wait_ge(wal_done, u + 1)
                    if u >= 2:
                        dve.wait_ge(wt_ps, 3 * (u - 1))
                    for qb in range(4):
                        c0, c1 = (P if qb == 0 else 0), (256 if qb == 3 else 384)
                        if u and qb == 3:
                            wa_probs(u - 1)
                        dve.wait_ge(sw_ps, 4 * u + qb + 1)
                        V.tensor_tensor_reduce(out=wa_p[:, u % 2, qb, c0:c1], in0=ps[:, 4 + qb, c0:c1],
                                               in1=walibi[:, u % 2, c0:c1], scale=1.0, scalar=-3e38,
                                               op0=ALU.add, op1=ALU.max,
                                               accum_out=mx[:, u % 2, qb:qb + 1]).then_inc(sw_done, 1)
                    dve.wait_ge(sw_done, 4 * u + 4)
                    V.tensor_scalar(nmx[:, u % 2, :], mx[:, u % 2, :], sink[:, u:u + 1], -1.0, ALU.max,
                                    ALU.mult).then_inc(wnm_done, 1)

            norm(3, memt, memn)
            norm_lo(3, mem_lo, mem_hi, MEMG, MEM)
            for n in range(PJ_XA, PJ_XA + 12):
                m = n - PJ_XA
                dve.wait_ge(pj_ps, n + 1)
                if m < 8:
                    V.tensor_copy(mkT[:, m, :], ps[:, n % 4, 0:MEM]).then_inc(pjD, 1)
                else:
                    t, half = (m - 8) % 2, (m - 8) // 2
                    V.tensor_copy(mv[:, t, half * 512:half * 512 + 512], ps[:, n % 4, :]).then_inc(pjD, 1)
            for u in range(XA_H + 2):
                if u < XA_H:
                    for qb in range(4):
                        dve.wait_ge(sx_ps, 4 * u + qb + 1)
                        V.tensor_reduce(nmx[:, u % 2, qb:qb + 1], ps[:, 4 + qb, 0:MEM], AX.X, ALU.max,
                                        negate=True).then_inc(xnm_done, 1)
                if 1 <= u <= XA_H:
                    h = u - 1
                    dve.wait_ge(xe1_done, 4 * h + 4)
                    link(V.reciprocal(rl[:, h % 2, :], lsum[:, h % 2, :]))
                    for qb in range(4):
                        v = xa_p[:, h % 2, qb, :]
                        last = V.tensor_scalar(v, v, rl[:, h % 2, qb:qb + 1], None, ALU.mult)
                    last.then_inc(ax_done, 1)
                if u >= 2:
                    h = u - 2
                    for i in range(2):
                        dve.wait_ge(xpv, 2 * h + i + 1)
                        V.tensor_copy(o_xa[:, 2 * h + i, :], ps[:, 2 + i, :]).then_inc(xO_ev, 1)

            for n in range(NB * KT):
                b, j = n // KT, n % KT
                if j == 0:
                    for k in range(KT):
                        dve.wait_ge(br_high, n + k + 1)
                        V.tensor_tensor(br_lo[:, k, :], (o_da, o_wa, o_xa)[b][:, k, :], br_hi[:, k, :].bitcast(f32),
                                        ALU.subtract).then_inc(br_low, 1)
                mv_ = merged[:, j, :]
                dve.wait_ge(gsig, n + 1)
                dve.wait_ge(g_ps, 4 * (n // 2) + n % 2 + 3)
                o = ps[:, 2 * (n % 4) + 1, :]
                if b == 0:
                    V.tensor_tensor(mv_, o, sg[:, n % 2, :], ALU.mult).then_inc(m_done, 1)
                else:
                    link(V.tensor_tensor(gtmp[:, n % 2, :], o, sg[:, n % 2, :], ALU.mult))
                    last = V.tensor_tensor(mv_, mv_, gtmp[:, n % 2, :], ALU.add)
                    if b == NB - 1:
                        link(last)
                        link(V.tensor_copy(mg_hi[:, j, :], mv_))
                        last = V.tensor_tensor(mg_lo[:, j, :], mv_, mg_hi[:, j, :].bitcast(f32), ALU.subtract)
                    last.then_inc(m_done, 1)
            residual(wo2_ps, x3_done, [(n // 4, n % 4) for n in range(8)], lambda t, half: 4 * half + t)

            norm(4, x, xn)
            norm_out(4, hT, FFN2G, S)
            dve.wait_ge(in_moe, 32)
            for t in range(TT):
                V.tensor_tensor(h2[:, t, :], xn[:, t, :], h2g, ALU.mult).then_inc(h2_done, 1)
            dve.wait_ge(rt_ps, 1)
            lps = ps[:, 4:4 + TT, 0:NE]
            link(V.tensor_reduce(small[:, 0:4], lps, AX.X, ALU.max))
            V.tensor_tensor(lg, lps, small[:, 0:4].unsqueeze(2).to_broadcast([P, TT, NE]),
                            ALU.subtract).then_inc(lg_done, 1)
            dve.wait_ge(lexp, 1)
            link(V.reduce_sum(small[:, 4:8], lg, AX.X))
            link(V.reciprocal(small[:, 8:12], small[:, 4:8]))
            V.tensor_tensor(aff, lg, small[:, 8:12].unsqueeze(2).to_broadcast([P, TT, NE]),
                            ALU.mult).then_inc(affd, 1)
            dve.wait_ge(affT_ps, 1)
            link(V.tensor_copy(affT, ps[0:NE, 5, :]))
            for r in range(8):
                left = wk if r else affT
                link(V.max(out=top[:, 8 * r:8 * r + 8], in_=left))
                if r < 7:
                    link(V.match_replace(out=wk, in_to_replace=top[:, 8 * r:8 * r + 8], in_values=left, imm_value=-1.0))
            least, count = top[:, CAP - 1:CAP], small[0:NE, 12:13]
            dve.wait_ge(slots_ready, 1)
            V.tensor_scalar(gt, affT, least, 0.0, ALU.is_gt, ALU.add, accum_out=count)
            link(V.tensor_scalar(eq, affT, least, None, ALU.is_equal))
            link(V.tensor_tensor_scan(cum, ones, eq, 0.0, ALU.mult, ALU.add))
            link(V.tensor_scalar(small[0:NE, 13:14], count, -1.0, float(CAP), ALU.mult, ALU.add))
            link(V.scalar_tensor_tensor(out=eq, in0=cum, scalar=small[0:NE, 13:14], in1=eq, op0=ALU.is_le, op1=ALU.mult))
            link(V.tensor_tensor(gt, gt, eq, ALU.add))
            link(V.tensor_tensor_scan(cum, ones, gt, 0.0, ALU.mult, ALU.add))
            V.tensor_tensor(wk, gt, cum, ALU.mult).then_inc(slot_d, 1)
            dve.wait_ge(slot_ps, 1)
            link(V.tensor_copy(slotT, ps[:, 6, 0:TT * NE].rearrange("p (t e) -> p t e", t=TT)))
            for t in range(TT):
                V.tensor_tensor(OH[:, t, :].rearrange("p (e c) -> p e c", e=NE),
                                iota1.unsqueeze(1).to_broadcast([P, NE, CAP]),
                                slotT[:, t, :].unsqueeze(2).to_broadcast([P, NE, CAP]),
                                ALU.is_equal).then_inc(oh_done, 1)
            dve.wait_ge(oh_done, TT)
            for t in range(2, TT):
                V.tensor_tensor(OHg[:, t, :].rearrange("p (e c) -> p e c", e=NE),
                                OH[:, t, :].rearrange("p (e c) -> p e c", e=NE),
                                aff[:, t, :].unsqueeze(2).to_broadcast([P, NE, CAP]),
                                ALU.mult).then_inc(ohgD_done, 1)

            dve.sem_inc(b67_free, 2)
            dve.sem_inc(ae_done, 2)
            dve.sem_inc(ye_done, 1)

            def tokens_out(q):
                for i in range(2):
                    dve.wait_ge(ga_ps, q * 2 + (i + 1))
                    V.tensor_copy(xeT[:, 4 * i:4 * i + 4, :].rearrange("p k c -> p (k c)"),
                                  ps[:, 6 + i, :]).then_inc(b67_free, 1)

            def turn(q, more, first=False):
                if not first:
                    V.tensor_copy(ohst, ohgT[:, q, :]).then_inc(st_done, 1)
                for a in range(2):
                    for i in range(2):
                        dve.wait_ge(sg_done, q * 4 + (2 * a + i + 1))
                        V.tensor_tensor(act_tok[64 * i:64 * i + 64, :],
                                        ps[64:128, 2 * i:2 * i + 2, :].rearrange("p b n -> p (b n)"),
                                        sg_e[64:128, i * 1024:i * 1024 + 1024], ALU.mult).then_inc(ae_done, 1)
                    for i in range(2):
                        dve.wait_ge(tr_ps, q * 4 + (2 * a + i + 1))
                        V.tensor_copy(act_e.rearrange("p (h j) c -> p j h c", h=2)[:, 4 * i:4 * i + 4, :, :],
                                      ps[:, 6 + i, :].rearrange("p (j h c) -> p j h c", j=4, h=2)).then_inc(b67_free, 1)
                    if a and more:
                        tokens_out(q + 1)
                    dve.wait_ge(e_chunks, q * ECH + (24 * a + 24))
                    V.tensor_copy(Y[64 * a:64 * a + 64, 0:512], ps[0:64, 4, :])
                    V.tensor_copy(Y[64 * a:64 * a + 64, 512:1024], ps[64:128, 4, :]).then_inc(ye_done, 1)
                    if first and a == 0:
                        for p in range(PAIRS):
                            dve.wait_ge(og_ps, p + 1)
                            V.tensor_copy(ohgT[:, p, :], ps[:, p % 4, :]).then_inc(og_ev, 1)
                        dve.wait_ge(og_ev, 1)
                        V.tensor_copy(ohst, ohgT[:, q, :]).then_inc(st_done, 1)
                for i in range(8):
                    t, half = i // 2, i % 2
                    xv = x[:, t, half * 512:half * 512 + 512]
                    dve.wait_ge(c_ps, q * 8 + (i + 1))
                    V.tensor_tensor(xv, ps[:, 6 + half, :], xv, ALU.add).then_inc(b67_free, 1)

            tokens_out(0)
            turn(0, True, first=True)
            with dve.Fori(1, PAIRS - 1) as q:
                turn(q, True)
            turn(PAIRS - 1, False)
            for t in range(TT):
                dve.wait_ge(f_rt, t + 1)
                link(V.reciprocal(rstd[:, t:t + 1], ssq[:, t:t + 1]))
                V.scalar_tensor_tensor(out=xn2[:, t, :], in0=x[:, t, :], scalar=rstd[:, t:t + 1], in1=fing,
                                       op0=ALU.mult, op1=ALU.mult).then_inc(o_done, 1)

        @block.tensor
        def _(pe):
            mm = nc.tensor.matmul
            at = [0]

            def take(k):
                i = at[0]
                at[0] += 1
                pe.wait_ge(w_split, i + 1)
                return tuple(v[:, i % 2, :].rearrange("p (k n) -> p k n", k=k) for v in (w_hi, w_lo))

            def to_features(o, h, ntok=S):
                w = take(KT)
                for k in range(KT):
                    mm(o, w[0][:, k, :], h[0][:, k, 0:ntok], start=(k == 0), stop=False)
                    mm(o, w[0][:, k, :], h[1][:, k, 0:ntok], start=False, stop=False)
                    last = mm(o, w[1][:, k, :], h[0][:, k, 0:ntok], start=False, stop=(k == KT - 1))
                return last

            def to_tokens(outs, toks, h, nk, signal, before=None):
                kk = HALF // outs[0].shape[-1]
                for k0 in range(0, nk, kk):
                    w = take(kk)
                    for t, o in enumerate(outs):
                        if k0 == 0 and before is not None:
                            before(t)
                        for k in range(k0, k0 + kk):
                            hi, lo = (toks(v, k, t) for v in h)
                            mm(o, hi, w[0][:, k - k0, :], start=(k == 0), stop=False)
                            mm(o, hi, w[1][:, k - k0, :], start=False, stop=False)
                            last = mm(o, lo, w[0][:, k - k0, :], start=False, stop=(k == nk - 1))
                        if k0 + kk == nk:
                            last.then_inc(signal, 1)
                    if k0 + kk < nk:
                        last.then_inc(w_used, 1)

            def tile_of(v, k, t):
                return v[:, k, t * P:(t + 1) * P]

            def norm_T(k, src, ntile):
                pe.wait_ge(n_xn, nbase[k + 1])
                for kb in range(KT):
                    if k == 0 and kb == 4:
                        pe.wait_ge(in_vec, 16 * 13)
                        for i, (c0, n) in enumerate(((0, 84), (84, 88), (172, 44), (216, 7))):
                            last = nc.tensor.transpose(ps[:, 7, c0:c0 + n], vrow[0:n, i, :], ident[0:n, 0:n])
                        last.then_inc(vec_ps, 1)
                    if kb >= 4:
                        pe.wait_ge(n_evD, 8 * k + kb - 3)
                    for t in range(ntile):
                        last = nc.tensor.transpose(ps[:, kb % 4, t * P:(t + 1) * P], src[:, t, kb * P:(kb + 1) * P], ident[:])
                    last.then_inc(n_tp, 1)

            def norm_ready(k):
                pe.wait_ge(n_evD, 8 * (k + 1))

            pe.wait_ge(consts, 1)
            norm_T(0, xn, TT)
            norm_ready(0)

            for g in range(GROUPS):
                if g:
                    pe.wait_ge(o_ev, 8 * g)
                for b in range(9):
                    n = 8 * g + b
                    if b < 8:
                        if n >= 4:
                            pe.wait_ge(qk_done, n - 3)
                        to_features(ps[:, n % 4, :], (h_hi, h_lo)).then_inc(qk_ps, 1)
                    if b:
                        m = n - 1
                        pe.wait_ge(sq_done, m + 1)
                        if m >= 2:
                            pe.wait_ge(rt_done, m - 1)
                        mm(ps[:, 6 + m % 2, :], mean64[:], sq[:, m % 2, :], start=True, stop=True).then_inc(ssq_ps, 1)

                def v_banks(t):
                    if t == 2:
                        pe.wait_ge(rt_done, 8 * (g + 1))

                to_tokens([ps[:, 4 + t, :] for t in range(TT)], tile_of if g == 0 else lambda v, k, t: v[:, k, t::4],
                          (h_hi, h_lo), KT, v_ps, v_banks)
                pe.wait_ge(qk_done, 8 * (g + 1))
                pe.wait_ge(v_ev, TT * (g + 1))
                for u in range(UB[g], UB[g + 1] + 2):
                    if u < UB[g + 1]:
                        _, h, tiles = units[u]
                        keys = k1_odd[:, h // 2, :] if h % 2 else qk[:, 4 + h // 2, :]
                        if u - 3 >= UB[g]:
                            pe.wait_ge(sm_done, u - 2)
                        for i, t in enumerate(tiles):
                            q = qk[:, h // 2, t * P:(t + 1) * P]
                            if g == 0:
                                for s in range(2):
                                    kb = max(t - 1 + s, 0)
                                    last = mm(ps[:, 4 + u % 3, (2 * i + s) * P:(2 * i + s + 1) * P], q,
                                              keys[:, kb * P:(kb + 1) * P], start=True, stop=True)
                            else:
                                last = mm(ps[:, 4 + u % 3, i * P:(i + 1) * P], q,
                                          keys[:, t * P:(t + 1) * P], start=True, stop=True)
                        last.then_inc(s_ps, 1)
                    m = u - 2
                    if m >= UB[g]:
                        _, h, tiles = units[m]
                        r = slice(64 * (h % 2), 64 * (h % 2) + 64)
                        pe.wait_ge(pt_done, m + 1)
                        if 8 * g + h >= 2:
                            pe.wait_ge(o_ev, 8 * g + h - 1)
                        for i, t in enumerate(tiles):
                            o = ps[r, 2 + h % 2, t * P:(t + 1) * P]
                            if g == 0:
                                for s in range(2):
                                    kb = max(t - 1 + s, 0)
                                    last = mm(o, v1[:, kb, h * DH:(h + 1) * DH], pt1[:, m % 2, (2 * i + s) * P:(2 * i + s + 1) * P],
                                              start=(s == 0), stop=(s == 1))
                            else:
                                last = mm(o, v1[:, t, h * DH:(h + 1) * DH], pt1[:, m % 2, i * P:(i + 1) * P], start=True, stop=True)
                        last.then_inc(pv_done, 1)
                    m = u - 1
                    if UB[g] <= m < UB[g + 1]:
                        pe.wait_ge(p_done, m + 1)
                        if m - 2 >= 0:
                            pe.wait_ge(pt_done, m - 1)
                        for i in range(4):
                            last = nc.tensor.transpose(ps[:, m % 2, i * P:(i + 1) * P], sm[:, m % 3, i * P:(i + 1) * P], ident[:])
                        last.then_inc(t_ps, 1)
            pe.wait_ge(o_ev, 24)
            for i in range(6):
                stat, g = (nm1, l1)[i // 3], i % 3
                for t in range(TT):
                    last = nc.tensor.transpose(ps[0:HEADS1, i, t * P:(t + 1) * P], stat[:, g, t, :], ident[:])
                last.then_inc(r_ps, 1)
            pe.wait_ge(coef_done, 1)
            for n in range(12):
                b, g = n // 3, n % 3
                if n >= 2:
                    pe.wait_ge(bc_done, n - 1)
                mm(ps[:, 6 + n % 2, :], selB[:, b, :], coef_all[:, g, :], start=True, stop=True).then_inc(bc_ps, 1)

            def out_proj(h, nk, sem_ps):
                for half in range(2):
                    to_tokens([ps[:, 4 * half + t, :] for t in range(TT)], tile_of, h, nk, sem_ps)

            pe.wait_ge(oT_low, 4)
            out_proj((oT_hi, oT_lo), 4, wo_ps)
            pe.wait_ge(x1_done, 8)

            norm_T(1, xn, TT)
            norm_ready(1)
            for j in range(FB):
                if j >= 2:
                    pe.wait_ge(conv_done, 4 * (j - 1))
                for i in range(2):
                    to_features(ps[:, 2 * (j % 2) + i, :], (h_hi, h_lo)).then_inc(f_ps, 1)
            pe.wait_ge(conv_done, 4 * FB)
            for f in range(FB):
                w = take(1)
                pe.wait_ge(act_done, f + 1)
                for t in range(TT):
                    for a_, w_ in ((act_hi, w[0]), (act_hi, w[1]), (act_lo, w[0])):
                        for half in range(2):
                            last = mm(ps[:, 2 * t + half, :], tile_of(a_, f, t), w_[:, 0, half * 512:half * 512 + 512],
                                      start=(f == 0 and a_ is act_hi and w_ is w[0]),
                                      stop=(f == FB - 1 and a_ is act_lo))
                            if f == FB - 1 and a_ is act_lo:
                                last.then_inc(dn_ps, 1)
                if f < FB - 1:
                    last.then_inc(w_used, 1)

            jobs = [0]

            def proj_T(nblk, h, ntok):
                for b in range(nblk):
                    n = jobs[0]
                    jobs[0] += 1
                    pj_bank_free(pe, n)
                    to_features(ps[:, n % 4, 0:ntok], h, ntok).then_inc(pj_ps, 1)

            def proj_tok(h, ntile, ncol):
                for half in range(max(ncol // 512, 1)):
                    n = jobs[0]
                    jobs[0] += ntile
                    to_tokens([ps[:, (n + t) % 4, 0:min(ncol, 512)] for t in range(ntile)], tile_of, h, KT, pj_ps,
                              lambda t: pj_bank_free(pe, n + t))

            pe.wait_ge(x2_done, 8)
            norm_T(2, xn, TT)
            norm_ready(2)
            proj_T(16, (h_hi, h_lo), S)
            proj_tok((h_hi, h_lo), TT, D)
            pj_all_done(pe, PJ_WA)

            def da_T(u):
                pe.wait_ge(a_done, u + 1)
                for i in range(2):
                    if u:
                        pe.wait_ge(dpt_done, 2 * (u - 1) + i + 1)
                    for kb in range(4):
                        last = nc.tensor.transpose(ps[:, i, kb * P:(kb + 1) * P], da_e[:, u % 2, 2 * i, kb * P:(kb + 1) * P], ident[:])
                    last.then_inc(dt_ps, 1)

            def da_pv(h):
                pe.wait_ge(dpt_done, 4 * h + 4)
                if h >= 2:
                    pe.wait_ge(dO_ev, h - 1)
                for kb in range(4):
                    last = mm(ps[:, 2 + h % 2, :], da_v[:, kb, h * P:(h + 1) * P], da_pt[:, 4 * (h % 2) + kb, :],
                              start=(kb == 0), stop=(kb == 3))
                last.then_inc(dpv, 1)

            for u in range(16 + 3):
                if u < 16:
                    for i in range(4):
                        h, qb, m = u // 2, 2 * (u % 2) + i // 2, i % 2
                        if u:
                            pe.wait_ge(sd_done, 4 * (u - 1) + i + 1)
                        mm(ps[:, 4 + i, :], da_q[:, h, qb * P:(qb + 1) * P], (da_k, da_k1)[m][:, h, :],
                           start=True, stop=True).then_inc(sd_ps, 1)
                if u >= 3 and u % 2:
                    da_pv((u - 3) // 2)
                if 1 <= u <= 16:
                    da_T(u - 1)

            pe.wait_ge(dO_ev, 8)
            for h in range(8):
                proj_T(1, (h_hi, h_lo), S)
                pe.wait_ge(on_sq, h + 1)
                if h >= 2:
                    pe.wait_ge(on_rt, h - 1)
                mm(ps[:, 4 + h % 2, :], mean128[:], da_e[:, 0, h % 2, :], start=True, stop=True).then_inc(on_ps, 1)
            proj_T(2, (h_hi, h_lo), S)
            proj_tok((h_hi, h_lo), TT, 256)
            pj_all_done(pe, PJ_XA)

            def wa_T(h):
                pe.wait_ge(aw_done, h + 1)
                for i in range(3):
                    m = 3 * h + i
                    if h:
                        pe.wait_ge(wpt_done, m - 2)
                    for j, (qb, kb) in enumerate(WA_BLOCKS[4 * i:4 * i + 4]):
                        c = (kb - qb + 1) * P
                        last = nc.tensor.transpose(ps[:, i, j * P:(j + 1) * P], wa_p[:, h % 2, qb, c:c + P], ident[:])
                    last.then_inc(wt_ps, 1)

            def wa_pv(h):
                r = slice(64 * (h % 2), 64 * (h % 2) + 64)
                kv = h // 4
                pe.wait_ge(wpt_done, 3 * h + 3)
                if h >= 2:
                    pe.wait_ge(wO_ev, h - 1)
                for n, (qb, kb) in enumerate(WA_BLOCKS):
                    last = mm(ps[r, 3, qb * P:(qb + 1) * P], wa_v[:, kb, kv * 64:kv * 64 + 64],
                              wa_pt[:, 10 * (h % 2) + n, :], start=(kb == WA_KB[qb][0]), stop=(kb == WA_KB[qb][-1]))
                last.then_inc(wpv, 1)

            for u in range(WA_H + 2):
                if u < WA_H:
                    for qb in range(4):
                        c0, c1 = (P if qb == 0 else 0), (256 if qb == 3 else 384)
                        k0 = (qb - 1) * P + c0
                        if u:
                            pe.wait_ge(sw_done, 4 * (u - 1) + qb + 1)
                        mm(ps[:, 4 + qb, c0:c1], wa_q[:, u // 2, qb * P:(qb + 1) * P], (wa_k, wa_k1)[u % 2][:, u // 4, k0:k0 + c1 - c0],
                           start=True, stop=True).then_inc(sw_ps, 1)
                if u >= 2:
                    wa_pv(u - 2)
                if 1 <= u <= WA_H:
                    wa_T(u - 1)

            pe.wait_ge(wO_ev, WA_H)
            norm_T(3, memn, MEM // P)
            norm_ready(3)
            proj_T(8, (mem_hi, mem_lo), MEM)
            proj_tok((mem_hi, mem_lo), MEM // P, D)
            proj_T(8, (h_hi, h_lo), S)
            pj_all_done(pe, PJ_XA + 20)
            for u in range(XA_H + 2):
                if u < XA_H:
                    for qb in range(4):
                        if u:
                            pe.wait_ge(xe1_done, 4 * (u - 1) + qb + 1)
                        for db in range(2):
                            last = mm(ps[:, 4 + qb, 0:MEM], xa_q[:, 2 * u + db, qb * P:(qb + 1) * P], mkT[:, 2 * u + db, :],
                                      start=(db == 0), stop=(db == 1))
                        last.then_inc(sx_ps, 1)
                if u >= 2:
                    h = u - 2
                    pe.wait_ge(xpt_done, 2 * h + 2)
                    for i in range(2):
                        if h:
                            pe.wait_ge(xO_ev, 2 * (h - 1) + i + 1)
                        for kb in range(2):
                            last = mm(ps[:, 2 + i, :], mv[:, kb, h * 256 + i * P:h * 256 + (i + 1) * P],
                                      xa_pt[:, 2 * (h % 2) + kb, :], start=(kb == 0), stop=(kb == 1))
                        last.then_inc(xpv, 1)
                if 1 <= u <= XA_H:
                    h = u - 1
                    pe.wait_ge(ax_done, h + 1)
                    for kb in range(2):
                        if h:
                            pe.wait_ge(xpt_done, 2 * (h - 1) + kb + 1)
                        for qb in range(4):
                            last = nc.tensor.transpose(ps[:, kb, qb * P:(qb + 1) * P], xa_p[:, h % 2, qb, kb * P:(kb + 1) * P], ident[:])
                        last.then_inc(xt_ps, 1)

            pe.wait_ge(xO_ev, 8)
            for m in range(NB * KT // 2):
                for i, h in enumerate(((h_hi, h_lo), (br_hi, br_lo))):
                    for n in (2 * m, 2 * m + 1):
                        if i == 0 and n >= 4:
                            pe.wait_ge(m_done, n - 3)
                        if i and n % KT == 0:
                            pe.wait_ge(br_low, n + KT)
                        to_features(ps[:, 2 * (n % 4) + i, :], h).then_inc(g_ps, 1)
            pe.wait_ge(m_done, NB * KT)
            out_proj((mg_hi, mg_lo), KT, wo2_ps)
            assert at[0] == NH
            pe.wait_ge(x3_done, 4)

            pe.wait_ge(n_xn, nbase[5])
            pe.wait_ge(in_small, 96)
            for kb in range(KT + 2):
                if kb < KT:
                    if kb >= 4:
                        pe.wait_ge(n_evD if kb % 2 else n_evA, 32 + (kb - 4) // 2 + 1)
                    for t in range(TT):
                        last = nc.tensor.transpose(ps[:, kb % 4, t * P:(t + 1) * P], xn[:, t, kb * P:(kb + 1) * P], ident[:])
                    last.then_inc(n_tp, 1)
                if kb >= 2:
                    k = kb - 2
                    pe.wait_ge(n_evD if k % 2 else n_evA, 32 + k // 2 + 1)
                    for t in range(TT):
                        last = mm(ps[:, 4 + t, 0:NE], hT[:, k, t * P:(t + 1) * P], wr[:, k, :],
                                  start=(k == 0), stop=(k == KT - 1))
            last.then_inc(rt_ps, 1)
            pe.wait_ge(affd, 1)
            for t in range(TT):
                last = nc.tensor.transpose(ps[0:NE, 5, t * P:(t + 1) * P], aff[:, t, :], ident[:])
            last.then_inc(affT_ps, 1)
            pe.wait_ge(slot_d, 1)
            for t in range(TT):
                last = nc.tensor.transpose(ps[:, 6, t * NE:(t + 1) * NE], wk[:, t * P:(t + 1) * P], ident[0:NE, 0:NE])
            last.then_inc(slot_ps, 1)
            pe.wait_ge(oh_done, TT)
            pe.wait_ge(h2_done, TT)

            def take_e(q, c):
                pe.wait_ge(landed[c % NS], q * (16 * ECH // NS) + 16 * (before[c % NS] + c // NS + 1))
                return ring[:, c % NS, :]

            def tokens_in(q, use):
                for i in range(2):
                    pe.wait_ge(b67_free, use + i)
                    for db in range(4):
                        for t in range(TT):
                            kb = 4 * i + db
                            last = mm(ps[:, 6 + i, db * P:(db + 1) * P], h2[:, t, kb * P:(kb + 1) * P],
                                      OH[:, t, bass.ds(q * P, P)], start=(t == 0), stop=(t == TT - 1))
                    last.then_inc(ga_ps, 1)

            def turn(q, more, first=False):
                for a in range(2):
                    if first and a:
                        pe.wait_ge(ohg_done, 2)
                        pe.wait_ge(ohgD_done, 2)
                        for p in range(PAIRS):
                            if p >= 4:
                                pe.wait_ge(og_ev, p - 3)
                            for t in range(TT):
                                last = nc.tensor.transpose(ps[:, p % 4, t * P:(t + 1) * P], OHg[:, t, p * P:(p + 1) * P], ident[:])
                            last.then_inc(og_ps, 1)
                        pe.wait_ge(og_ev, PAIRS)
                    pe.wait_ge(ae_done, q * 4 + (2 * a + 2))
                    for k in range(KT):
                        ws = [take_e(q, 24 * a + 2 * k), take_e(q, 24 * a + 2 * k + 1)]
                        for c in range(4):
                            for i, w in enumerate(ws):
                                last = mm(ps[64 * i:64 * i + 64, c, :], xeT[:, k, a * CAP:(a + 1) * CAP],
                                          w[:, c * 512:c * 512 + 512], start=(k == 0), stop=(k == KT - 1))
                                if c == 3:
                                    last.then_inc(e_chunks, 1)
                    for i in range(2):
                        pe.wait_ge(b67_free, q * SEQ + (2 * a + i + 3))
                        if i == 0:
                            pe.wait_ge(ae_done, q * 4 + (2 * a + 4))
                        for j in range(4):
                            f = 4 * i + j
                            last = nc.tensor.transpose(ps[:, 6 + i, j * P:(j + 1) * P], act_tok[:, f * P:(f + 1) * P], ident[:])
                        last.then_inc(tr_ps, 1)
                    if a and more:
                        tokens_in(q + 1, q * SEQ + 7)
                    pe.wait_ge(b67_free, q * SEQ + (2 * a + 6))
                    pe.wait_ge(ye_done, q * 2 + (a + 1))
                    for k in range(8):
                        w = take_e(q, 24 * a + 16 + k)
                        for j in range(2):
                            f = 2 * k + j
                            for half in range(2):
                                last = mm(ps[64 * half:64 * half + 64, 4, :], act_e[:, f, :],
                                          w[:, j * D + half * 512:j * D + half * 512 + 512],
                                          start=(f == 0), stop=(f == FT - 1))
                        last.then_inc(e_chunks, 1)
                if more:
                    pe.wait_ge(b67_free, q * SEQ + 10)
                pe.wait_ge(st_done, q + 1)
                pe.wait_ge(ye_done, q * 2 + 3)
                for i in range(8):
                    t, half = i // 2, i % 2
                    pe.wait_ge(b67_free, q * SEQ + (i + (9 if more else 7)))
                    mm(ps[:, 6 + half, :], ohst[:, t * P:(t + 1) * P], Y[:, half * 512:half * 512 + 512],
                       start=True, stop=True).then_inc(c_ps, 1)

            tokens_in(0, 1)
            pe.wait_ge(b67_free, 4)
            turn(0, True, first=True)
            with pe.Fori(1, PAIRS - 1) as q:
                turn(q, True)
            turn(PAIRS - 1, False)


_INS = ["x", "mixer_norm", "ffn_norm", "attn_w_in", "attn_q_gain", "attn_k_gain", "attn_w_out",
        "ffn_w_up", "ffn_conv_w", "ffn_conv_b", "ffn_w_down", "mem_2", "attn_norm_g_2", "mem_norm_g_2",
        "w_in_2", "w_mem_kv_2", "da_lambda_q1_2", "da_lambda_k1_2", "da_lambda_q2_2", "da_lambda_k2_2",
        "da_subln_g_2", "wa_sink_2", "w_da_o_2", "w_wa_o_2", "w_xa_o_2", "w_out_2", "ffn_norm_g_2",
        "w_router_2", "w_exp_gate_2", "w_exp_up_2", "w_exp_down_2", "final_norm_g_2"]


def kernel(**inputs):
    import numpy as np
    import concourse.bacc as bacc
    from concourse import mybir
    from concourse.bass_utils import run_bass_kernel_spmd

    nc = bacc.Bacc("TRN2", target_bir_lowering=False, num_devices=1)
    arrays, aps = {}, {}
    for name in _INS:
        a = np.ascontiguousarray(inputs[name])
        arrays["in_" + name] = a
        aps[name] = nc.dram_tensor("in_" + name, a.shape, mybir.dt.from_np(a.dtype), kind="ExternalInput").ap()
    out = nc.dram_tensor("out_0", (1, S, D), mybir.dt.float32, kind="ExternalOutput").ap()
    build(nc, aps, out)
    r = run_bass_kernel_spmd(nc, [arrays], core_ids=[0])
    return r.results[0]["out_0"]
```
